# Optimizing a Trainium2 kernel written in Bass

```python
import math
import jax, jax.numpy as jnp
from jax import lax
import numpy as np

D_MODEL = 1024
BATCH = 1
SEQ = 1024
DEPTH = 1

CHUNK = 64
N_MEM = 256
QBLK = 128

HEAD_DIM = 64
GROUP_W = D_MODEL // 4
D_MIX = 4 * GROUP_W

DIFF_HEADS = GROUP_W // HEAD_DIM
DIFF_QK = HEAD_DIM // 2
CONV_CH = GROUP_W
CONV_K = 31
SWA_HEADS = GROUP_W // HEAD_DIM
SWA_KV_HEADS = max(1, SWA_HEADS // 2)
SWA_WINDOW = 128
SWA_WINDOW_CHUNKS = SWA_WINDOW // CHUNK
FOX_HEADS = GROUP_W // HEAD_DIM

IN_SIZES = (DIFF_HEADS * 2 * DIFF_QK, DIFF_HEADS * 2 * DIFF_QK, DIFF_HEADS * HEAD_DIM,
            2 * CONV_CH,
            SWA_HEADS * HEAD_DIM, SWA_KV_HEADS * HEAD_DIM, SWA_KV_HEADS * HEAD_DIM,
            FOX_HEADS * HEAD_DIM, FOX_HEADS * HEAD_DIM, FOX_HEADS * HEAD_DIM, FOX_HEADS)
N_IN = sum(IN_SIZES)

X_HEADS = 4
X_HEAD_DIM = D_MODEL // X_HEADS

N_EXPERTS = 64
N_GROUPS = 8
TOPK_GROUPS = 4
TOP_K = 6
D_EXPERT = D_MODEL // 4
N_SHARED = 1
D_SHARED = N_SHARED * D_EXPERT
ROUTED_SCALE = 2.5
EXPERT_BLOCK = 128

DEEPNORM_ALPHA = (2 * DEPTH) ** 0.25
DEEPNORM_BETA = (8 * DEPTH) ** -0.25
LN_EPS = 1e-5

kernel_name = 'hybrid_streaming_headgroup_moe_encoder'

F32 = jnp.float32

def layer_norm(x, g, b):
    xf = x.astype(F32)
    mu = xf.mean(-1, keepdims=True)
    var = jnp.square(xf - mu).mean(-1, keepdims=True)
    return ((xf - mu) * lax.rsqrt(var + LN_EPS) * g.astype(F32) + b.astype(F32)).astype(x.dtype)

def to_qblocks(t):
    b, h, s, d = t.shape
    return t.reshape(b, h, s // QBLK, QBLK, d).transpose(2, 0, 1, 3, 4)

def from_qblocks(o):
    nb, b, h, q, d = o.shape
    return o.transpose(1, 0, 3, 2, 4).reshape(b, nb * q, h, d)

def diff_attention(aq, ak, av, lq1, lk1, lq2, lk2, subln_g, lambda_init):
    b, s, _ = aq.shape
    q = aq.reshape(b, s, DIFF_HEADS, 2, DIFF_QK).transpose(3, 0, 2, 1, 4)
    k = ak.reshape(b, s, DIFF_HEADS, 2, DIFF_QK).transpose(3, 0, 2, 1, 4)
    v = av.reshape(b, s, DIFF_HEADS, HEAD_DIM).transpose(0, 2, 1, 3)
    lam = (jnp.exp(jnp.sum(lq1.astype(F32) * lk1.astype(F32)))
           - jnp.exp(jnp.sum(lq2.astype(F32) * lk2.astype(F32))) + lambda_init)
    scale = DIFF_QK ** -0.5
    kchunk = jnp.arange(s) // CHUNK
    k1, k2 = k[0], k[1]

    def block(args):
        q1b, q2b, qchunk = args
        mask = kchunk[None, :] <= qchunk[:, None]
        s1 = jnp.einsum('bhqd,bhkd->bhqk', q1b, k1).astype(F32) * scale
        s2 = jnp.einsum('bhqd,bhkd->bhqk', q2b, k2).astype(F32) * scale
        p1 = jax.nn.softmax(jnp.where(mask, s1, -jnp.inf), axis=-1)
        p2 = jax.nn.softmax(jnp.where(mask, s2, -jnp.inf), axis=-1)
        return jnp.einsum('bhqk,bhkd->bhqd', (p1 - lam * p2).astype(v.dtype), v)

    o = lax.map(block, (to_qblocks(q[0]), to_qblocks(q[1]), kchunk.reshape(-1, QBLK)))
    o = from_qblocks(o).astype(F32)
    o = o * lax.rsqrt(jnp.mean(o * o, -1, keepdims=True) + LN_EPS) * subln_g.astype(F32)
    return (o * (1.0 - lambda_init)).reshape(b, s, DIFF_HEADS * HEAD_DIM).astype(av.dtype)

def conformer_conv(u, conv_w, conv_b, ln_g, ln_b):
    a, gate = jnp.split(u, 2, axis=-1)
    z = a * jax.nn.sigmoid(gate)
    w = conv_w.astype(z.dtype)[:, None, :]
    z = lax.conv_general_dilated(z, w, window_strides=(1,), padding=[(CONV_K - 1, 0)],
                                 dimension_numbers=('NWC', 'WIO', 'NWC'),
                                 feature_group_count=CONV_CH)
    z = z + conv_b.astype(z.dtype)
    z = layer_norm(z, ln_g, ln_b)
    return jax.nn.silu(z)

def sliding_window_attention(sq, sk, sv, sink):
    b, s, _ = sq.shape
    nc = s // CHUNK
    g = SWA_HEADS // SWA_KV_HEADS
    q = sq.reshape(b, nc, CHUNK, SWA_KV_HEADS, g, HEAD_DIM)
    k = sk.reshape(b, nc, CHUNK, SWA_KV_HEADS, HEAD_DIM)
    v = sv.reshape(b, nc, CHUNK, SWA_KV_HEADS, HEAD_DIM)

    def band(t):
        parts = [jnp.pad(t[:, :nc - j], ((0, 0), (j, 0), (0, 0), (0, 0), (0, 0)))
                 for j in range(SWA_WINDOW_CHUNKS - 1, -1, -1)]
        return jnp.concatenate(parts, axis=2)

    kb, vb = band(k), band(v)
    slot_offset = (SWA_WINDOW_CHUNKS - 1) - jnp.arange(SWA_WINDOW_CHUNKS * CHUNK) // CHUNK
    valid = jnp.arange(nc)[:, None] >= slot_offset[None, :]
    sc = jnp.einsum('bcqhgd,bckhd->bchgqk', q, kb).astype(F32) * (HEAD_DIM ** -0.5)
    sc = jnp.where(valid[None, :, None, None, None, :], sc, -jnp.inf)
    snk = sink.astype(F32).reshape(SWA_KV_HEADS, g)[None, None, :, :, None, None]
    m = jnp.maximum(sc.max(-1, keepdims=True), snk)
    e = jnp.exp(sc - m)
    p = e / (e.sum(-1, keepdims=True) + jnp.exp(snk - m))
    o = jnp.einsum('bchgqk,bckhd->bcqhgd', p.astype(sv.dtype), vb)
    return o.reshape(b, s, SWA_HEADS * HEAD_DIM)

def forgetting_attention(fq, fk, fv, f_logit, f_bias):
    b, s, _ = fq.shape
    q = fq.reshape(b, s, FOX_HEADS, HEAD_DIM).transpose(0, 2, 1, 3)
    k = fk.reshape(b, s, FOX_HEADS, HEAD_DIM).transpose(0, 2, 1, 3)
    v = fv.reshape(b, s, FOX_HEADS, HEAD_DIM).transpose(0, 2, 1, 3)
    logf = jax.nn.log_sigmoid(f_logit.astype(F32) + f_bias.astype(F32))
    cum = jnp.cumsum(logf, axis=1).transpose(0, 2, 1)
    pos = jnp.arange(s)
    scale = HEAD_DIM ** -0.5

    def block(args):
        qb, cq, qpos = args
        sc = (jnp.einsum('bhqd,bhkd->bhqk', qb, k).astype(F32) * scale
              + cq[..., None] - cum[:, :, None, :])
        sc = jnp.where(pos[None, :] <= qpos[:, None], sc, -jnp.inf)
        p = jax.nn.softmax(sc, axis=-1)
        return jnp.einsum('bhqk,bhkd->bhqd', p.astype(v.dtype), v)

    cqb = cum.reshape(b, FOX_HEADS, s // QBLK, QBLK).transpose(2, 0, 1, 3)
    o = lax.map(block, (to_qblocks(q), cqb, pos.reshape(-1, QBLK)))
    return from_qblocks(o).reshape(b, s, FOX_HEADS * HEAD_DIM)

def hybrid_mixer(h, w_in, lq1, lk1, lq2, lk2, subln_g, conv_w, conv_b, conv_ln_g, conv_ln_b,
                 swa_sink, fox_fb, w_out, lambda_init):
    proj = h @ w_in
    cuts = [int(c) for c in np.cumsum(IN_SIZES)[:-1]]
    aq, ak, av, cu, sq, sk, sv, fq, fk, fv, ff = jnp.split(proj, cuts, axis=-1)
    ya = diff_attention(aq, ak, av, lq1, lk1, lq2, lk2, subln_g, lambda_init)
    yb = conformer_conv(cu, conv_w, conv_b, conv_ln_g, conv_ln_b)
    yc = sliding_window_attention(sq, sk, sv, swa_sink)
    yd = forgetting_attention(fq, fk, fv, ff, fox_fb)
    return jnp.concatenate([ya, yb, yc, yd], axis=-1) @ w_out

def memory_cross_attention(h, mem, xq, xkv, xo):
    b, s, _ = h.shape
    q = (h @ xq).reshape(b, s, X_HEADS, X_HEAD_DIM)
    k, v = jnp.split(mem @ xkv, 2, axis=-1)
    k = k.reshape(b, -1, X_HEADS, X_HEAD_DIM)
    v = v.reshape(b, -1, X_HEADS, X_HEAD_DIM)
    sc = jnp.einsum('bshd,bmhd->bhsm', q, k).astype(F32) * (X_HEAD_DIM ** -0.5)
    p = jax.nn.softmax(sc, axis=-1)
    o = jnp.einsum('bhsm,bmhd->bshd', p.astype(v.dtype), v).reshape(b, s, D_MODEL)
    return o @ xo

def moe_ffn(h, router_w, router_bias, wg, wu, wd, sg, su, sd):
    b, s, d = h.shape
    t = b * s
    xf = h.reshape(t, d)
    scores = jax.nn.sigmoid((xf @ router_w).astype(F32))
    choice = scores + router_bias.astype(F32)
    per_group = N_EXPERTS // N_GROUPS
    group_score = lax.top_k(choice.reshape(t, N_GROUPS, per_group), 2)[0].sum(-1)
    _, gidx = lax.top_k(group_score, TOPK_GROUPS)
    gmask = jax.nn.one_hot(gidx, N_GROUPS, dtype=F32).sum(1) > 0
    choice = jnp.where(jnp.repeat(gmask, per_group, axis=1), choice, -jnp.inf)
    _, eidx = lax.top_k(choice, TOP_K)
    gate = jnp.take_along_axis(scores, eidx, axis=1)
    gate = gate / gate.sum(-1, keepdims=True) * ROUTED_SCALE

    n = t * TOP_K
    flat_e = eidx.reshape(n)
    flat_tok = jnp.repeat(jnp.arange(t), TOP_K)
    order = jnp.argsort(flat_e)
    se, st, sgate = flat_e[order], flat_tok[order], gate.reshape(n)[order]
    counts = jnp.bincount(flat_e, length=N_EXPERTS)
    padded = (counts + EXPERT_BLOCK - 1) // EXPERT_BLOCK * EXPERT_BLOCK
    start = jnp.cumsum(counts) - counts
    pend = jnp.cumsum(padded)
    pstart = pend - padded
    dest = pstart[se] + jnp.arange(n) - start[se]
    nb = -(-n // EXPERT_BLOCK) + N_EXPERTS
    npad = nb * EXPERT_BLOCK
    buf_tok = jnp.full((npad,), t, jnp.int32).at[dest].set(st)
    buf_gate = jnp.zeros((npad,), h.dtype).at[dest].set(sgate.astype(h.dtype))
    blk_exp = jnp.minimum(jnp.searchsorted(pend, jnp.arange(nb) * EXPERT_BLOCK, side='right'),
                          N_EXPERTS - 1)
    x_pad = jnp.concatenate([xf, jnp.zeros((1, d), xf.dtype)], axis=0)

    def expert_block(args):
        rows, g, e = args
        xb = x_pad[rows]
        hb = jax.nn.silu(xb @ wg[e]) * (xb @ wu[e])
        return (hb @ wd[e]) * g[:, None]

    yb = lax.map(expert_block, (buf_tok.reshape(nb, EXPERT_BLOCK),
                                buf_gate.reshape(nb, EXPERT_BLOCK), blk_exp))
    routed = jnp.zeros((t + 1, d), h.dtype).at[buf_tok].add(yb.reshape(npad, d))[:t]
    shared = (jax.nn.silu(xf @ sg) * (xf @ su)) @ sd
    return (routed + shared).reshape(b, s, d)

def setup_inputs(seed: int = 0) -> dict:
    key = jax.random.key(seed)
    ks = jax.random.split(key, 40)
    L = DEPTH

    def nrm(i, shape, scale):
        return jax.random.normal(ks[i], shape, F32) * scale

    def gain(i, shape):
        return 1.0 + nrm(i, shape, 0.02)

    return {
        'x': nrm(0, (BATCH, SEQ, D_MODEL), 1.0),
        'mem': nrm(1, (BATCH, N_MEM, D_MODEL), 1.0),
        'ln_in_g': gain(2, (D_MODEL,)),
        'ln_in_b': nrm(3, (D_MODEL,), 0.02),
        'w_in': nrm(4, (L, D_MODEL, N_IN), D_MODEL ** -0.5),
        'diff_lq1': nrm(5, (L, DIFF_QK), 0.1),
        'diff_lk1': nrm(6, (L, DIFF_QK), 0.1),
        'diff_lq2': nrm(7, (L, DIFF_QK), 0.1),
        'diff_lk2': nrm(8, (L, DIFF_QK), 0.1),
        'diff_subln_g': gain(9, (L, HEAD_DIM)),
        'conv_w': nrm(10, (L, CONV_K, CONV_CH), CONV_K ** -0.5),
        'conv_b': nrm(11, (L, CONV_CH), 0.02),
        'conv_ln_g': gain(12, (L, CONV_CH)),
        'conv_ln_b': nrm(13, (L, CONV_CH), 0.02),
        'swa_sink': nrm(14, (L, SWA_HEADS), 0.5),
        'fox_fb': 2.0 + nrm(15, (L, FOX_HEADS), 0.5),
        'w_out': nrm(16, (L, D_MIX, D_MODEL), D_MIX ** -0.5 * DEEPNORM_BETA),
        'ln1_g': gain(17, (L, D_MODEL)),
        'ln1_b': nrm(18, (L, D_MODEL), 0.02),
        'xq': nrm(19, (L, D_MODEL, D_MODEL), D_MODEL ** -0.5),
        'xkv': nrm(20, (L, D_MODEL, 2 * D_MODEL), D_MODEL ** -0.5),
        'xo': nrm(21, (L, D_MODEL, D_MODEL), D_MODEL ** -0.5 * DEEPNORM_BETA),
        'ln2_g': gain(22, (L, D_MODEL)),
        'ln2_b': nrm(23, (L, D_MODEL), 0.02),
        'router_w': nrm(24, (L, D_MODEL, N_EXPERTS), D_MODEL ** -0.5),
        'router_bias': nrm(25, (L, N_EXPERTS), 0.01),
        'exp_wg': nrm(26, (L, N_EXPERTS, D_MODEL, D_EXPERT), D_MODEL ** -0.5),
        'exp_wu': nrm(27, (L, N_EXPERTS, D_MODEL, D_EXPERT), D_MODEL ** -0.5),
        'exp_wd': nrm(28, (L, N_EXPERTS, D_EXPERT, D_MODEL), D_EXPERT ** -0.5 * DEEPNORM_BETA),
        'sh_wg': nrm(29, (L, D_MODEL, D_SHARED), D_MODEL ** -0.5),
        'sh_wu': nrm(30, (L, D_MODEL, D_SHARED), D_MODEL ** -0.5),
        'sh_wd': nrm(31, (L, D_SHARED, D_MODEL), D_SHARED ** -0.5 * DEEPNORM_BETA),
        'ln3_g': gain(32, (L, D_MODEL)),
        'ln3_b': nrm(33, (L, D_MODEL), 0.02),
    }

def reference(x, mem, ln_in_g, ln_in_b, w_in, diff_lq1, diff_lk1, diff_lq2, diff_lk2,
              diff_subln_g, conv_w, conv_b, conv_ln_g, conv_ln_b, swa_sink, fox_fb, w_out,
              ln1_g, ln1_b, xq, xkv, xo, ln2_g, ln2_b, router_w, router_bias,
              exp_wg, exp_wu, exp_wd, sh_wg, sh_wu, sh_wd, ln3_g, ln3_b):
    h = layer_norm(x, ln_in_g, ln_in_b)
    for l in range(DEPTH):
        lambda_init = 0.8 - 0.6 * math.exp(-0.3 * l)
        mix = hybrid_mixer(h, w_in[l], diff_lq1[l], diff_lk1[l], diff_lq2[l], diff_lk2[l],
                           diff_subln_g[l], conv_w[l], conv_b[l], conv_ln_g[l], conv_ln_b[l],
                           swa_sink[l], fox_fb[l], w_out[l], lambda_init)
        h = layer_norm(DEEPNORM_ALPHA * h + mix, ln1_g[l], ln1_b[l])
        xa = memory_cross_attention(h, mem, xq[l], xkv[l], xo[l])
        h = layer_norm(DEEPNORM_ALPHA * h + xa, ln2_g[l], ln2_b[l])
        ff = moe_ffn(h, router_w[l], router_bias[l], exp_wg[l], exp_wu[l], exp_wd[l],
                     sh_wg[l], sh_wu[l], sh_wd[l])
        h = layer_norm(DEEPNORM_ALPHA * h + ff, ln3_g[l], ln3_b[l])
    return h


_drawn_inputs = setup_inputs


def setup_inputs(seed=0):
    import zlib

    import numpy as np

    out = dict(_drawn_inputs(seed))
    spreads = {}
    factors = {'diff_lq2': 3.665,
     'diff_lk2': 7.165,
     'diff_subln_g': 2.84,
     'conv_ln_g': 3.028,
     'conv_ln_b': 3.864,
     'swa_sink': 64.0,
     'fox_fb': 39.176,
     'ln3_g': 7.506,
     'ln3_b': 7.791}
    for name, (base, spread) in spreads.items():
        noise = np.random.default_rng([zlib.crc32(name.encode()), seed]).standard_normal(out[name].shape)
        drawn = base * np.exp(spread * noise) if base else spread * noise
        out[name] = __import__('jax').numpy.asarray(drawn.astype(out[name].dtype))
    for name, factor in factors.items():
        out[name] = (out[name] * factor).astype(out[name].dtype)
    return out
```

```python
from contextlib import ExitStack

import concourse.bass as bass
from concourse import mybir

F32 = mybir.dt.float32
BF16 = mybir.dt.bfloat16
I32 = mybir.dt.int32
ACT = mybir.ActivationFunctionType
ALU = mybir.AluOpType
AX = mybir.AxisListType

P = 128
S = 1024
D = 1024
NT = S // P
KD = D // P
HALF = 512
CHUNK = 64
N_MEM = 256
CONV_K = 31
PAD = CONV_K - 1
X_HEADS = 4
N_EXP = 64
N_GRP = 8
PER_GRP = N_EXP // N_GRP
TOP_GRP = 4
TOP_K = 6
D_EXP = 256
EXP_BLOCK = 128
MAX_BLOCKS = (S * TOP_K) // EXP_BLOCK + N_EXP
LN_EPS = 1e-5
ALPHA = 2.0 ** 0.25
LAMBDA_INIT = 0.2
ROUTED_SCALE = 2.5
NEG = -1e30
SENTINEL = -3e38
TAKEN = 3e38

C_AQ, C_AK, C_AV, C_CU = 0, 256, 512, 768
C_SQ, C_SK, C_SV = 1280, 1536, 1664
C_FQ, C_FK, C_FV, C_FF = 1792, 2048, 2304, 2560
N_IN = 2564

R_LN = {"in": (0, 8), "1": (16, 24), "2": (32, 40)}
R_CONVB, R_CLNG, R_CLNB, R_SUBG, R_CONVW = 48, 50, 52, 54, 55
N_ROWS = R_CONVW + 2 * CONV_K

DIFF_STEPS = 2 * NT * 2
FOX_LOG_AT = DIFF_STEPS + 14
U = 1024


def attention_steps():
    steps = []
    for group, kind, pairs in ((0, "diff", [0]), (1, "diff", [1]), (2, "swa", [0, 1]),
                               (3, "fox", [0]), (4, "fox", [1])):
        for pair in pairs:
            for tile in range(NT):
                for parity in range(2):
                    steps.append((group, kind, pair, parity, tile))
    return steps


def key_tiles(kind, tile):
    return list(range(max(0, tile - 1), tile + 1)) if kind == "swa" else list(range(tile + 1))


def make_plan():
    steps = attention_steps()
    proj = {
        0: [("q", 0), ("k", 0), ("v", 0, 0), ("v", 0, 1)],
        1: [("q", 1), ("k", 1)],
        2: [("q", 2), ("q", 3), ("k", 2), ("v", 2, 0)],
        3: [("q", 4), ("k", 4), ("v", 4, 0), ("v", 4, 1), ("v", 4, 2), ("v", 4, 3)],
        4: [("q", 5), ("k", 5)],
    }
    plan = [("proj", ("a", 0)), ("proj", ("g", 0)), ("proj", ("a", 1)), ("proj", ("g", 1))]
    plan += [("proj", p) for p in proj[0] + proj[1]]
    starts = {g: next(n for n, step in enumerate(steps) if step[0] == g) for g in range(5)}
    at = {}
    for g in range(2, 5):
        for n, p in enumerate(proj[g]):
            at[starts[g - 1] + 2 + (2 if len(proj[g]) > 2 else 5) * n] = ("proj", p)
    at[FOX_LOG_AT + 3] = ("cum", "cum")
    for s in range(len(steps) + 2):
        if s in at:
            plan.append(at[s])
        if s >= 2:
            plan.append(("turn", s - 2))
        if s < len(steps):
            plan.append(("scores", s))
        if s >= 2:
            plan.append(("values", s - 2))
    return steps, plan


def build(nc, ins, out, h_res, h_table, acc):
    STEPS, PLAN = make_plan()
    NS = len(STEPS)
    item_of, n_items = {}, 0
    for kind, what in PLAN:
        if kind in ("proj", "cum"):
            item_of[what] = n_items
            n_items += 1
        elif kind == "scores":
            for m in range(2 if STEPS[what][1] == "diff" else 1):
                item_of[("s", what, m)] = n_items
                n_items += 1
    ATT_ITEMS = n_items
    GROUP_READY = {0: item_of[("v", 0, 1)], 1: item_of[("k", 1)], 2: item_of[("v", 2, 0)],
                   3: item_of[("v", 4, 3)], 4: item_of[("k", 5)]}
    LN_CHUNKS = 2 * KD
    chunk_of, n_chunks = {}, 1 + LN_CHUNKS
    for s, (_, kind, _, _, tile) in enumerate(STEPS):
        nk = len(key_tiles(kind, tile))
        chunk_of[s] = n_chunks
        n_chunks += (nk + 3) // 4
    ATT_CHUNKS = n_chunks
    CH_LN = {("in", 0): 1, ("in", 1): 1 + KD, ("1", 0): ATT_CHUNKS}
    CH_MEM = ATT_CHUNKS + KD
    CH_LN["1", 1] = CH_MEM + 4
    CH_X = CH_LN["1", 1] + KD
    CH_LN["2", 0] = CH_X + 16
    CH_LN["2", 1] = CH_LN["2", 0] + KD
    CH_ROUTE = CH_LN["2", 1] + KD
    CH_MOE = CH_ROUTE + 1
    IT_MEM = ATT_ITEMS
    IT_XQ = IT_MEM + 4
    IT_X = IT_XQ + 8
    X_ORDER = [("xs", 0)]
    for u in range(8):
        if u + 1 < 8:
            X_ORDER.append(("xs", u + 1))
        X_ORDER.append(("xo", u))
    x_item = {w: IT_X + n for n, w in enumerate(X_ORDER)}
    IT_ROUTE = IT_X + 16
    IT_SH = IT_ROUTE + 1

    with ExitStack() as ctx:
        def sb(name, shape, dt=F32):
            return ctx.enter_context(nc.sbuf_tensor(name, shape, dt))

        def sem(name):
            return ctx.enter_context(nc.semaphore(name))

        W_SLOT = KD * 260
        N_W = 3
        arena = sb("arena", [P, 42 * U + 64 + 640 + N_W * W_SLOT])
        at = [0]

        def cut(n):
            a = arena[:, at[0]:at[0] + n]
            at[0] += n
            return a

        hT = cut(8 * U).rearrange("p (k s) -> p k s", k=KD)
        yT_flat = cut(8 * U)
        yT = yT_flat.rearrange("p (k s) -> p k s", k=KD)
        qkv0 = cut(8 * U)
        qkv1 = cut(8 * U)
        probs_flat = cut(4 * U)
        pT_flat = cut(2 * U)
        conv_flat = cut(4 * U + 64)
        misc = cut(640)
        w_ring = cut(N_W * W_SLOT).rearrange("p (n c) -> p n c", n=N_W)
        gb = sb("gb", [P, 2 * U])

        Q = [r[:, 0:4 * U].rearrange("p (m s) -> p m s", m=4) for r in (qkv0, qkv1)]
        K = [r[:, 4 * U:6 * U].rearrange("p (m s) -> p m s", m=2) for r in (qkv0, qkv1)]
        V = [r[:, 6 * U:8 * U].rearrange("p (t c) -> p t c", t=NT) for r in (qkv0, qkv1)]
        xnorm = {"in": yT_flat.rearrange("p (t d) -> p t d", t=NT),
                 "1": qkv0.rearrange("p (t d) -> p t d", t=NT),
                 "2": qkv0.rearrange("p (t d) -> p t d", t=NT),
                 "3": qkv0.rearrange("p (t d) -> p t d", t=NT)}
        big_w = qkv1.rearrange("p (k c) -> p k c", k=KD)
        probs = probs_flat.rearrange("p (n m s) -> p n m s", n=2, m=2)
        probsT = pT_flat.rearrange("p (n k q) -> p n k q", n=2, k=8)
        z = conv_flat[:, 0:2 * (S + PAD)].rearrange("p (c s) -> p c s", c=2)
        zc = conv_flat[:, 2 * (S + PAD):2 * (S + PAD) + 2 * S].rearrange("p (c s) -> p c s", c=2)
        res_tmp = pT_flat.rearrange("p (n d) -> p n d", n=2)
        tri_ones = misc[:, 0:640]

        ident = sb("ident", [P, P])
        ident_b = sb("ident_b", [P, P], BF16)
        mask_chunk = sb("mask_chunk", [P, P], BF16)
        mask_causal = sb("mask_causal", [P, P], BF16)
        mask_prev = sb("mask_prev", [P, P], BF16)
        rows = conv_flat[:, 0:P]
        sig = probs_flat.rearrange("p (c s) -> p c s", c=4)
        cols = sb("cols", [P, N_ROWS])
        lamv = probs_flat[:, 3 * U + P:3 * U + 2 * P].rearrange("p (n c) -> p n c", n=4)
        lam = sb("lam", [P, 8])
        sink = sb("sink", [P, 4])
        nsink = sb("nsink", [P, 4])
        foxb = sb("foxb", [P, 4])
        subg = sb("subg", [P, 1])
        blk_ones = probs_flat[:, 3 * U:3 * U + P]
        cln_x = probs_flat[:, 0:2 * U].rearrange("p (h n c) -> p h n c", h=2, n=4)
        squares = pT_flat.rearrange("p (c s) -> p c s", c=2)
        root = conv_flat[:, 0:2 * U].rearrange("p (c s) -> p c s", c=2)
        mem_nat = conv_flat[:, 0:2 * U].rearrange("p (n d) -> p n d", n=2)
        memT = probs_flat[:, 0:2 * U].rearrange("p (k m) -> p k m", k=KD)
        kmT = conv_flat[:, 0:2 * U].rearrange("p (k m) -> p k m", k=KD)
        vm = conv_flat[:, 2 * U:4 * U].rearrange("p (n d) -> p n d", n=2)
        qxT = qkv0.rearrange("p (k s) -> p k s", k=KD)
        xprobs = probs_flat[:, 2 * U:4 * U].rearrange("p (n t m) -> p n t m", n=2, t=4)
        xprobsT = pT_flat.rearrange("p (n m q) -> p n m q", n=2, m=2)
        stats = sb("stats", [P, NT, 2, 6])
        mv = sb("mv", [P, NT, 2])
        rstd = sb("rstd", [P, NT])
        negm = sb("negm", [P, 2, 2])
        sums = sb("sums", [P, 2, 2])
        rsum = sb("rsum", [P, 2, 4])
        xneg, xsum = sb("xneg", [P, 2, 4]), sb("xsum", [P, 2, 4])
        logf = sb("logf", [P, 2, NT, 4])
        fstat = gb[:, 0:NT * P].rearrange("p (t c) -> p t c", t=NT)
        cumT = gb[:, U:2 * U]

        psum = ctx.enter_context(nc.psum_tensor("psum", [P, 8, 512], F32))
        wide = [psum[:, 2 * n:2 * n + 2, :].rearrange("p a b -> p (a b)") for n in range(2)]
        ptb = [psum[:, 4 + n, :] for n in range(2)]
        obank = psum[:, 6, :]
        sbank = psum[:, 7, :]

        x_loaded = [sem(f"x_loaded{t}") for t in range(NT)]
        rows_loaded = sem("rows_loaded")
        params_loaded = sem("params_loaded")
        gb_loaded = sem("gb_loaded")
        w_loaded = [sem(f"w_loaded{n}") for n in range(N_W)]
        consts_ready = sem("consts_ready")
        pool_step = sem("pool_step")
        q_zeroed = sem("q_zeroed")
        dve_step = sem("dve_step")
        act_step = sem("act_step")
        ln_stat = sem("ln_stat")
        ln_std = sem("ln_std")
        ln_done = sem("ln_done")
        res_ready = sem("res_ready")
        res_stored = [sem(f"res_stored{n}") for n in range(2)]
        wide_full = sem("wide_full")
        wide_read = sem("wide_read")
        pt_full = sem("pt_full")
        pt_copied = sem("pt_copied")
        row_max = sem("row_max")
        probs_ready = sem("probs_ready")
        pv_done = sem("pv_done")
        o_read = sem("o_read")
        glu_done = sem("glu_done")
        lam_sum = sem("lam_sum")
        lam_exp = sem("lam_exp")
        fox_z = sem("fox_z")
        fox_e = sem("fox_e")
        fox_l = sem("fox_l")
        fstat_ready = sem("fstat_ready")
        cum_full = sem("cum_full")
        aug_ready = sem("aug_ready")
        bigw_loaded = sem("bigw_loaded")

        w_in = ins["w_in"].rearrange("o (k p) n -> p (o k) n", p=P)
        xq = ins["xq"].rearrange("o (k p) n -> p (o k) n", p=P)
        xkv = ins["xkv"].rearrange("o (k p) n -> p (o k) n", p=P)

        def slot_view(n, width):
            return w_ring[:, n, 0:KD * width].rearrange("p (k c) -> p k c", k=KD)

        w_loads = []
        use_of = {}

        def add_load(width, parts, users):
            for u in users:
                use_of[u] = len(w_loads)
            w_loads.append((width, parts))

        def cols_of(src, c, n):
            return src[:, :, c:c + n]

        for c in range(2):
            add_load(256, [(0, 128, cols_of(w_in, C_CU + 128 * c, 128)),
                           (128, 128, cols_of(w_in, C_CU + 256 + 128 * c, 128))], [("a", c), ("g", c)])
        add_load(256, [(0, 128, cols_of(w_in, C_AQ, 128)), (128, 128, cols_of(w_in, C_AK, 128))],
                 [("q", 0), ("k", 0)])
        add_load(256, [(0, 256, cols_of(w_in, C_AV, 256))], [("v", 0, 0), ("v", 0, 1)])
        add_load(256, [(0, 128, cols_of(w_in, C_AQ + 128, 128)), (128, 128, cols_of(w_in, C_AK + 128, 128))],
                 [("q", 1), ("k", 1)])
        add_load(256, [(0, 64, cols_of(w_in, C_SQ, 64)), (64, 64, cols_of(w_in, C_SQ + 128, 64)),
                       (128, 64, cols_of(w_in, C_SQ + 64, 64)), (192, 64, cols_of(w_in, C_SQ + 192, 64))],
                 [("q", 2), ("q", 3)])
        add_load(256, [(0, 256, cols_of(w_in, C_SK, 256))], [("k", 2), ("v", 2, 0)])
        add_load(256, [(0, 128, cols_of(w_in, C_FQ, 128)), (128, 128, cols_of(w_in, C_FK, 128))],
                 [("q", 4), ("k", 4)])
        add_load(260, [(0, 260, cols_of(w_in, C_FV, 260))], [("v", 4, n) for n in range(4)])
        add_load(256, [(0, 128, cols_of(w_in, C_FQ + 128, 128)), (128, 128, cols_of(w_in, C_FK + 128, 128))],
                 [("q", 5), ("k", 5)])
        for n in range(8):
            add_load(256, [(0, 256, cols_of(xkv, 256 * n, 256))], [("m", n)])
        for n in range(4):
            add_load(256, [(0, 256, cols_of(xq, 256 * n, 256))], [("xq", 2 * n), ("xq", 2 * n + 1)])
        add_load(256, [(0, 256, ins["sh_wg"].rearrange("o (k p) n -> p (o k) n", p=P))], [("sg", 0), ("sg", 1)])
        add_load(256, [(0, 256, ins["sh_wu"].rearrange("o (k p) n -> p (o k) n", p=P))], [("su", 0), ("su", 1)])
        add_load(256, [(0, 256, None)], [("sd", 0)])

        all_items = dict(item_of)
        for n in range(8):
            all_items[("m", n)] = IT_MEM + n // 2
            all_items[("xq", n)] = IT_XQ + n
        for m in range(2):
            all_items[("sg", m)] = IT_SH + 2 * m
            all_items[("su", m)] = IT_SH + 2 * m + 1
        last_item = [max(all_items[u] for u in use_of if use_of[u] == n) for n in range(len(w_loads) - 1)]
        RMS_OF = {}
        n_max = 0
        for s in range(NS):
            for m in range(2 if STEPS[s][1] == "diff" else 1):
                RMS_OF[(s, m)] = n_max
                n_max += 1
        SLOT_OF = {0: 0, 1: 1, 2: 0, 3: 1, 4: 0}
        Q_ZEROED = {0: 1, 1: 2, 2: 3, 3: 4, 4: 5}
        Y_CHUNK = {"diff": 0, "swa": 4, "fox": 6}
        VAL = {"diff": V[0], "swa": V[1], "fox": V[0]}
        assert 2 * CONV_K < NS

        w_count, per_slot = [], [0] * N_W
        for n, (_, parts) in enumerate(w_loads):
            per_slot[n % N_W] += 16 * len(parts)
            w_count.append(per_slot[n % N_W])

        conv_done = sem("conv_done")
        cln_full, cln_stat, cln_std, cln_xn = sem("cln_full"), sem("cln_stat"), sem("cln_std"), sem("cln_xn")
        cln_back, cln_act = sem("cln_back"), sem("cln_act")
        sq_ready, rms_full, rms_root, rms_done = sem("sq_ready"), sem("rms_full"), sem("rms_root"), sem("rms_done")
        mem_loaded = sem("mem_loaded")
        mix_full, mix_read = sem("mix_full"), sem("mix_read")
        xmax, xprobs_ready = sem("xmax"), sem("xprobs_ready")
        rw_loaded, bias_loaded = sem("rw_loaded"), sem("bias_loaded")
        logits_read, routed = sem("logits_read"), sem("routed")
        rank_full, blk_full = sem("rank_full"), sem("blk_full")
        table_ready = sem("table_ready")
        hs_ready = sem("hs_ready")
        acc_stored = sem("acc_stored")
        h_stored = sem("h_stored")
        out_stored = sem("out_stored")
        gu_loaded = [sem(f"gu_loaded{n}") for n in range(2)]
        wd_loaded = [sem(f"wd_loaded{n}") for n in range(2)]
        onehot_ready, idx_full, idx_ready = sem("onehot_ready"), sem("idx_full"), sem("idx_ready")
        gathered = [sem(f"gathered{n}") for n in range(2)]
        xt_full, xt_copied = sem("xt_full"), sem("xt_copied")
        gu_full, silu_done, h_ready = sem("gu_full"), sem("silu_done"), sem("h_ready")
        ht_full, ht_copied = sem("ht_full"), sem("ht_copied")
        y_full, y_ready, scattered = sem("y_full"), sem("y_ready"), sem("scattered")
        moe_setup, moe_step = sem("moe_setup"), sem("moe_step")
        pool_pace, out_step = sem("pool_pace"), sem("out_step")

        rw = misc[:, 0:KD * N_EXP].rearrange("p (k e) -> p k e", k=KD)
        rbias = misc[:, KD * N_EXP:KD * N_EXP + N_EXP]
        logitsT = probs_flat[0:N_EXP, 0:U]
        hs = yT_flat[:, 6 * U:8 * U].rearrange("p (k s) -> p k s", k=2)
        hs_tmp = probs_flat[:, U:2 * U]
        r_all = conv_flat
        rs_scores = r_all[:, 0:512].rearrange("p (t e) -> p t e", t=NT)
        rs_choice = r_all[:, 512:512 + NT * 66].rearrange("p (t e) -> p t e", t=NT)
        rs_sel = r_all[:, 1040:1552].rearrange("p (t e) -> p t e", t=NT)
        rs_gate = r_all[:, 1552:2064].rearrange("p (t e) -> p t e", t=NT)
        rs_tmp = r_all[:, 2064:2576].rearrange("p (t e) -> p t e", t=NT)
        rs_rank = r_all[:, 2576:3088].rearrange("p (t e) -> p t e", t=NT)
        rs_off = r_all[:, 3088:3088 + 576].rearrange("p (t e) -> p t e", t=NT + 1)
        rs_selb = r_all[:, 3664:3920].bitcast(BF16).rearrange("p (t e) -> p t e", t=NT)
        small = pT_flat[:, U:2 * U]
        top8 = small[:, 0:512].rearrange("p (t g n) -> p t g n", t=NT, g=N_GRP)
        gsum = small[:, 512:608].rearrange("p (t g) -> p t g", t=NT)
        gtop = small[:, 608:672].rearrange("p (t g) -> p t g", t=NT)
        gpen = small[:, 672:736].rearrange("p (t g) -> p t g", t=NT)
        gden = small[:, 736:752].rearrange("p (t g) -> p t g", t=NT)
        nb_i = small[:, 752:816].bitcast(I32)
        nb_f = small[:, 816:1008].rearrange("p (n e) -> p n e", n=3)
        tri_b = sb("tri_b", [P, P], BF16)
        ones_b = sb("ones_b", [P, P], BF16)
        iota_s = sb("iota_s", [P, P])
        pcol = sb("pcol", [P, 4])
        blk_exp = sb("blk_exp", [P, 1])
        table = qkv1[0:1, 7 * U + 768:8 * U].bitcast(I32)
        dest = qkv1[:, 6 * U:6 * U + 512].rearrange("p (e t) -> p e t", e=N_EXP)
        gparts = qkv1[:, 7 * U:7 * U + 768].bitcast(BF16).rearrange("p (e t g) -> p e t g", e=N_EXP, t=NT)
        onehot = conv_flat[:, 0:U].bitcast(BF16).rearrange("p (n t r) -> p n t r", n=2, t=NT)
        h_exp = conv_flat[:, U:U + 512].rearrange("p (n f) -> p n f", n=2)
        hT_exp = conv_flat[:, U + 512:2 * U].rearrange("p (n k r) -> p n k r", n=2, k=2)
        xg = probs_flat[:, 0:2 * U].rearrange("p (n d) -> p n d", n=2)
        xgT = probs_flat[:, 2 * U:4 * U].rearrange("p (n k r) -> p n k r", n=2, k=KD)
        y_exp = pT_flat.rearrange("p (n d) -> p n d", n=2)
        slot_cols = sb("slot_cols", [P, 2, NT, 6], BF16)
        d8 = sb("d8", [P, NT])
        blk_base = sb("blk_base", [P, 1])
        idx_new = sb("idx_new", [P, 2], I32)
        gate_new = sb("gate_new", [P, 2])
        idx_now = sb("idx_now", [P, 2], I32)
        gate_now = sb("gate_now", [P, 2])
        idx_tmp = sb("idx_tmp", [P, 2, 2])
        exp_w = [r[:, 0:6 * U] for r in (qkv1, yT_flat)]
        gu_w = [r[:, 0:4 * U].rearrange("p (k c) -> p k c", k=KD) for r in exp_w]
        wd_w = [r[:, 4 * U:6 * U].rearrange("p (k c) -> p k c", k=2) for r in exp_w]
        MAX_TURNS = (MAX_BLOCKS + 1) // 2

        block = ctx.enter_context(nc.Block())

        def bcast(name, n):
            return ins[name].rearrange("(o n) -> o n", o=1).broadcast_to([P, n]) \
                if len(ins[name].shape) == 1 else ins[name].broadcast_to([P, n])

        @block.sync
        def _(sp):
            x_dram = ins["x"].rearrange("b (t p) d -> t p (b d)", p=P)
            res_dram = h_res.rearrange("(t p) d -> t p d", p=P)
            table_dram = h_table.rearrange("(t p) d -> t p d", p=P)
            acc_dram = acc.rearrange("(t p) d -> t p d", p=P)
            out_dram = out.rearrange("b (t p) d -> t p (b d)", p=P)
            for t in range(2):
                sp.dma_start(xnorm["in"][:, t, :], x_dram[t]).then_inc(x_loaded[t], 16)
            def param_rows(row, src):
                sp.dma_start(rows[row:row + src.shape[0], 0:src.shape[1]], src).then_inc(rows_loaded, 16)

            for r, g, b in ((0, "ln_in_g", "ln_in_b"), (16, "ln1_g", "ln1_b"), (32, "ln2_g", "ln2_b")):
                for row, name in ((r, g), (r + 8, b)):
                    src = ins[name]
                    src = src.rearrange("(k p) -> k p", p=P) if len(src.shape) == 1 \
                        else src.rearrange("o (k p) -> (o k) p", p=P)
                    param_rows(row, src)
            for row, name in ((R_CONVB, "conv_b"), (R_CLNG, "conv_ln_g"), (R_CLNB, "conv_ln_b")):
                param_rows(row, ins[name].rearrange("o (k p) -> (o k) p", p=P))
            for half in range(2):
                sp.dma_start(rows[R_SUBG:R_SUBG + 1, 64 * half:64 * half + 64],
                             ins["diff_subln_g"]).then_inc(rows_loaded, 16)
            for c in range(2):
                param_rows(R_CONVW + CONV_K * c, ins["conv_w"][0, :, P * c:P * c + P])
            for t in range(2, NT):
                sp.dma_start(xnorm["in"][:, t, :], x_dram[t]).then_inc(x_loaded[t], 16)
            for n, name in enumerate(("diff_lq1", "diff_lk1", "diff_lq2", "diff_lk2")):
                sp.dma_start(lamv[:, n, :], bcast(name, 32)).then_inc(params_loaded, 16)
            sp.dma_start(sink[:, :], bcast("swa_sink", 4)).then_inc(params_loaded, 16)
            sp.dma_start(foxb[:, :], bcast("fox_fb", 4)).then_inc(params_loaded, 16)

            def load_gb(g, b):
                sp.dma_start(gb[:, 0:U], bcast(g, D)).then_inc(gb_loaded, 16)
                sp.dma_start(gb[:, U:2 * U], bcast(b, D)).then_inc(gb_loaded, 16)

            load_gb("ln_in_g", "ln_in_b")

            def store_residual(ln):
                for t in range(NT):
                    sp.wait_ge(res_ready, NT * ln + t + 1)
                    sp.dma_start(res_dram[t], res_tmp[:, t % 2, :]).then_inc(res_stored[t % 2], 16)

            def load_residual(ln):
                for n in range(2):
                    sp.wait_ge(res_stored[n], 16 * ln * NT // 2)
                for t in range(NT):
                    sp.dma_start(xnorm[str(ln)][:, t, :], res_dram[t]).then_inc(x_loaded[t], 16)

            def load_w(n):
                width, parts = w_loads[n]
                if n >= N_W:
                    sp.wait_ge(wide_full, last_item[n - N_W] + 1)
                if n == len(w_loads) - 1:
                    sp.dma_start(w_ring[:, n % N_W, 0:2 * D].rearrange("p (k c) -> p k c", k=2),
                                 ins["sh_wd"].rearrange("o (k p) c -> p (o k) c", p=P)
                                 ).then_inc(w_loaded[n % N_W], 16)
                    return
                for c, m, src in parts:
                    sp.dma_start(slot_view(n % N_W, width)[:, :, c:c + m], src).then_inc(w_loaded[n % N_W], 16)

            for n in range(N_W):
                load_w(n)
            store_residual(0)
            for n in range(N_W, 10):
                load_w(n)
            first4 = STEPS.index((4, "fox", 1, 0, 0))
            sp.wait_ge(pv_done, first4)
            sp.dma_start(big_w, ins["w_out"].rearrange("o (k p) c -> p (o k) c", p=P)).then_inc(bigw_loaded, 16)
            sp.wait_ge(aug_ready, 2)
            load_gb("ln1_g", "ln1_b")
            sp.wait_ge(pv_done, NS)
            load_residual(1)
            for n in range(10, 12):
                load_w(n)
            sp.wait_ge(rms_done, 2)
            for n in range(2):
                sp.dma_start(mem_nat[:, n, :], ins["mem"][0, P * n:P * n + P, :]).then_inc(mem_loaded, 16)
            load_w(12)
            sp.wait_ge(mix_full, NT)
            sp.dma_start(big_w, ins["xo"].rearrange("o (k p) c -> p (o k) c", p=P)).then_inc(bigw_loaded, 16)
            store_residual(1)
            for n in range(13, 22):
                load_w(n)
            load_gb("ln2_g", "ln2_b")
            sp.dma_start(rw[:, :, :], ins["router_w"].rearrange("o (k p) e -> p (o k) e", p=P)).then_inc(rw_loaded, 16)
            sp.dma_start(rbias, bcast("router_bias", N_EXP)).then_inc(rw_loaded, 16)
            sp.wait_ge(wide_full, x_item[("xs", 7)] + 1)
            load_residual(2)
            for n in range(22, 25):
                load_w(n)
            for t in range(NT):
                sp.wait_ge(res_ready, NT * 2 + t + 1)
                sp.dma_start(table_dram[t], xnorm["2"][:, t, :]).then_inc(h_stored, 16)
            for t in range(NT):
                sp.wait_ge(mix_read, 2 * NT + t + 1)
                sp.dma_start(acc_dram[t], xnorm["2"][:, t, :]).then_inc(acc_stored, 16)

            exp_gu = [ins[n].rearrange("o e (k p) f -> (o e) p k f", p=P) for n in ("exp_wg", "exp_wu")]
            exp_d = ins["exp_wd"].rearrange("o e (k p) c -> (o e) p k c", p=P)

            def load_expert(e, slot):
                for n in range(2):
                    sp.dma_start(gu_w[slot][:, :, D_EXP * n:D_EXP * n + D_EXP],
                                 exp_gu[n][bass.ds(e, 1)].rearrange("o p k f -> p (o k) f")
                                 ).then_inc(gu_loaded[slot], 16)

            def load_expert_down(e, slot):
                sp.dma_start(wd_w[slot], exp_d[bass.ds(e, 1)].rearrange("o p k c -> p (o k) c")
                             ).then_inc(wd_loaded[slot], 16)

            sp.wait_ge(table_ready, 1)
            sp.wait_ge(mix_full, 3 * NT)
            for j in range(2):
                e = sp.value_load(table[0:1, j:j + 1], min_val=0, max_val=N_EXP - 1)
                load_expert(e, j)
                load_expert_down(e, j)
            turns = sp.value_load(table[0:1, P:P + 1], min_val=1, max_val=MAX_TURNS)
            with sp.Fori(0, turns) as i:
                for b in range(2):
                    e = sp.value_load(table[0:1, bass.ds(2 * i + 2 + b, 1)], min_val=0, max_val=N_EXP - 1)
                    sp.wait_ge(gu_full, 2 * i + b + 1)
                    load_expert(e, b)
                    sp.wait_ge(y_full, 2 * i + b + 1)
                    load_expert_down(e, b)
            for b in range(2):
                sp.wait_ge(gu_loaded[b], 32 * turns + 32)
                sp.wait_ge(wd_loaded[b], 16 * turns + 16)
            load_gb("ln3_g", "ln3_b")
            sp.wait_ge(scattered, 32 * turns + 32)
            for t in range(NT):
                sp.dma_start(xnorm["3"][:, t, :], acc_dram[t]).then_inc(x_loaded[t], 16)
            for t in range(NT):
                sp.wait_ge(res_ready, NT * 3 + t + 1)
                sp.dma_start(out_dram[t], xnorm["3"][:, t, :]).then_inc(out_stored, 16)
            sp.wait_ge(out_stored, 16 * NT)

        @block.gpsimd
        def _(pool):
            chain = [0]

            def link(made):
                chain[0] += 1
                made.then_inc(pool_step, 1)
                pool.wait_ge(pool_step, chain[0])

            def select(t, fill, pattern, mult, op, base=0):
                return nc.gpsimd.affine_select(out=t, in_=t, pattern=pattern, compare_op=op,
                                               fill=fill, base=base, channel_multiplier=mult)

            link(nc.gpsimd.memset(ident[:, :], 0.0))
            link(select(ident[:, :], 1.0, [[-1, P]], 1, ALU.not_equal))
            nc.gpsimd.tensor_copy(ident_b[:, :], ident[:, :]).then_inc(consts_ready, 1)
            link(nc.gpsimd.memset(mask_causal[:, :], 0.0))
            select(mask_causal[:, :], NEG, [[-1, P]], 1, ALU.is_ge).then_inc(consts_ready, 1)
            link(nc.gpsimd.memset(mask_chunk[:, :], 0.0))
            nc.gpsimd.memset(mask_chunk[0:CHUNK, CHUNK:P], NEG).then_inc(consts_ready, 1)
            link(nc.gpsimd.memset(mask_prev[:, :], NEG))
            nc.gpsimd.memset(mask_prev[0:CHUNK, CHUNK:P], 0.0).then_inc(consts_ready, 1)
            nc.gpsimd.memset(qkv0[:, 0:4 * U], 0.0).then_inc(q_zeroed, 1)
            nc.gpsimd.memset(qkv1[:, 0:4 * U], 0.0).then_inc(q_zeroed, 1)
            def residual(ln, staged):
                pool.wait_ge(gb_loaded, 32 * (ln + 1))
                if staged:
                    link(nc.gpsimd.tensor_scalar(gb[:, :], gb[:, :], ALPHA, None, ALU.mult))
                src = xnorm["in"] if ln == 0 else xnorm[str(ln)]
                for t in range(NT):
                    pool.wait_ge(ln_done, NT * ln + t + 1)
                    if staged:
                        if NT * ln + t >= 2:
                            pool.wait_ge(res_stored[t % 2], 16 * ((NT * ln + t) // 2))
                        dst = res_tmp[:, t % 2, :]
                    else:
                        dst = src[:, t, :]
                    link(nc.gpsimd.tensor_tensor(dst, src[:, t, :], gb[:, 0:U], ALU.mult))
                    nc.gpsimd.tensor_tensor(dst, dst, gb[:, U:2 * U], ALU.add).then_inc(res_ready, 1)

            residual(0, True)
            link(nc.gpsimd.memset(tri_ones, 1.0))
            select(tri_ones[:, 0:P], 0.0, [[1, P]], -1, ALU.is_ge).then_inc(consts_ready, 1)
            for group, q in ((2, 4), (3, 4), (4, 2)):
                prev = [s for s in range(NS) if STEPS[s][0] == group - 2]
                pool.wait_ge(wide_full, item_of[("s", prev[-1], 1 if group - 2 < 2 else 0)] + 1)
                region = (qkv0, qkv1)[SLOT_OF[group]]
                zero = nc.gpsimd.memset(region[:, 0:q * U], 0.0)
                if group == 2:
                    zero.then_inc(q_zeroed, 1)
                else:
                    link(zero)
                    link(nc.gpsimd.memset(region[:, 4 * U:6 * U], 0.0))
                    for p in range(2):
                        row = (64, 0)[p]
                        link(nc.gpsimd.memset(Q[SLOT_OF[group]][row + 32:row + 33, p, :], 1.0))
                        link(nc.gpsimd.memset(K[SLOT_OF[group]][row:row + 1, p, :], 1.0))
                    pool.sem_inc(q_zeroed, 1)
            link(nc.gpsimd.memset(tri_b[:, :], 1.0))
            select(tri_b[:, :], 0.0, [[1, P]], -1, ALU.is_gt).then_inc(consts_ready, 1)
            nc.gpsimd.memset(ones_b[:, :], 1.0).then_inc(consts_ready, 1)
            nc.gpsimd.iota(iota_s[:, :], [[1, P]], base=0, channel_multiplier=0,
                           allow_small_or_imprecise_dtypes=True).then_inc(consts_ready, 1)
            for n, (base, mult) in enumerate(((0, 1), (-S, -1), (S, 1))):
                nc.gpsimd.iota(pcol[:, n:n + 1], [[0, 1]], base=base, channel_multiplier=mult,
                               allow_small_or_imprecise_dtypes=True).then_inc(consts_ready, 1)
            for b in range(2):
                nc.gpsimd.iota(slot_cols[:, b, :, 0], [[P, NT]], base=0, channel_multiplier=0,
                               allow_small_or_imprecise_dtypes=True).then_inc(consts_ready, 1)
                nc.gpsimd.iota(slot_cols[:, b, :, 1], [[0, NT]], base=0, channel_multiplier=1,
                               allow_small_or_imprecise_dtypes=True).then_inc(consts_ready, 1)
                nc.gpsimd.memset(slot_cols[:, b, :, 2], 1.0).then_inc(consts_ready, 1)
            pool.wait_ge(rms_full, 2)
            residual(1, True)
            pool.wait_ge(pt_full, CH_LN["2", 1] + KD)
            residual(2, False)

            pool.wait_ge(moe_setup, 1)
            pool.dma_start(h_table[S:S + P, :], y_exp[:, 0, :]).then_inc(scattered, 16)
            pool.wait_ge(scattered, 16)
            pool.dma_start(acc[S:S + P, :], y_exp[:, 0, :]).then_inc(scattered, 16)
            pool.wait_ge(scattered, 32)
            pool.wait_ge(h_stored, 16 * NT)
            pool.wait_ge(acc_stored, 16 * NT)

            def gather(slot, wait):
                pool.indirect_dma_start(xg[:, slot, :], None, h_table[:, :],
                                        bass.IndirectOffsetOnAxis(ap=idx_new[:, slot:slot + 1], axis=0)
                                        ).then_inc(gathered[slot], 16)

            for j in range(2):
                pool.wait_ge(idx_ready, j + 1)
                gather(j, None)
            turns = pool.value_load(table[0:1, P:P + 1], min_val=1, max_val=MAX_TURNS)
            with pool.Fori(0, turns) as i:
                for b in range(2):
                    pool.wait_ge(idx_ready, 2 * i + b + 3)
                    pool.sem_inc(pool_pace, 1)
                    pool.wait_ge(xt_full, 4 * i + 2 * b + 2)
                    pool.sem_inc(pool_pace, 1)
                    gather(b, None)
                    pool.wait_ge(scattered, 32 * i + 16 * b + 32)
                    pool.sem_inc(pool_pace, 1)
                    pool.wait_ge(y_ready, 2 * i + b + 2)
                    pool.sem_inc(pool_pace, 1)
                    pool.indirect_dma_start(acc[:, :], bass.IndirectOffsetOnAxis(ap=idx_now[:, b:b + 1], axis=0),
                                            y_exp[:, b, :], None, compute_op=ALU.add).then_inc(scattered, 16)
            pool.wait_ge(scattered, 32 * turns + 32)
            pool.sem_inc(pool_pace, 1)
            for b in range(2):
                pool.wait_ge(gathered[b], 16 * turns + 16)
                pool.sem_inc(pool_pace, 1)
            pool.wait_ge(gb_loaded, 128)
            for t in range(NT):
                pool.wait_ge(ln_done, NT * 3 + t + 1)
                nc.gpsimd.tensor_tensor(xnorm["3"][:, t, :], xnorm["3"][:, t, :], gb[:, 0:U],
                                        ALU.mult).then_inc(out_step, 1)
                pool.wait_ge(out_step, t + 1)
                nc.gpsimd.tensor_tensor(xnorm["3"][:, t, :], xnorm["3"][:, t, :], gb[:, U:2 * U],
                                        ALU.add).then_inc(res_ready, 1)

        @block.tensor
        def _(pe):
            def transposes(chunk, blocks):
                if chunk >= 2:
                    pe.wait_ge(pt_copied, chunk - 1)
                for dst, src in blocks:
                    mm = nc.tensor.transpose(dst, src, ident[0:src.shape[0], 0:src.shape[0]])
                mm.then_inc(pt_full, 1)

            pe.wait_ge(rows_loaded, 16 * 13)
            pe.wait_ge(pool_step, 2)
            pe.wait_ge(consts_ready, 4)
            transposes(0, [(ptb[0][:, 0:N_ROWS], rows[0:N_ROWS, :])])

            def ln_transposes(which, half, done):
                pe.wait_ge(ln_done, done)
                for k in range(KD):
                    c = CH_LN[which, half] + k
                    transposes(c, [(ptb[c % 2][:, P * n:P * n + P],
                                    xnorm[which][:, 4 * half + n, P * k:P * k + P]) for n in range(4)])

            for half in range(2):
                ln_transposes("in", half, 4 * half + 4)

            def weights(what):
                load = use_of[what]
                pe.wait_ge(w_loaded[load % N_W], w_count[load])
                return slot_view(load % N_W, w_loads[load][0])

            def transposed_projection(dst, w, c0, m=P):
                for half in range(2):
                    for k in range(KD):
                        mm = nc.tensor.matmul(dst[0:m, HALF * half:HALF * half + HALF], w[:, k, c0:c0 + m],
                                              hT[:, k, HALF * half:HALF * half + HALF],
                                              start=(k == 0), stop=(k == KD - 1))
                return mm

            def projection(what):
                item = item_of[what]
                w = weights(what)
                if what == ("a", 0):
                    pe.wait_ge(pt_copied, 1 + LN_CHUNKS)
                if item >= 2:
                    pe.wait_ge(wide_read, item - 1)
                dst = wide[item % 2]
                if what[0] == "v":
                    if what[1] == 0:
                        tiles, n0, n, stride = range(4 * what[2], 4 * what[2] + 4), 0, 256, 256
                    elif what[1] == 2:
                        tiles, n0, n, stride = range(NT), 128, 128, 128
                    else:
                        tiles, n0, n, stride = range(2 * what[2], 2 * what[2] + 2), 0, 260, 512
                    for a, t in enumerate(tiles):
                        for k in range(KD):
                            mm = nc.tensor.matmul(dst[:, a * stride:a * stride + n], hT[:, k, P * t:P * t + P],
                                                  w[:, k, n0:n0 + n], start=(k == 0), stop=(k == KD - 1))
                else:
                    second = what[0] == "g" or (what[0] == "k" and what[1] != 2) or what == ("q", 3)
                    mm = transposed_projection(dst, w, P if second else 0)
                mm.then_inc(wide_full, 1)

            def scores(s):
                group, kind, pair, parity, tile = STEPS[s]
                keys = key_tiles(kind, tile)
                slot = SLOT_OF[group]
                pe.wait_ge(wide_read, GROUP_READY[group] + 1)
                if kind == "fox":
                    pe.wait_ge(aug_ready, group - 2)
                for m in range(2 if kind == "diff" else 1):
                    item = item_of[("s", s, m)]
                    pe.wait_ge(wide_read, item - 1)
                    dst = wide[item % 2]
                    if kind == "diff":
                        q, k = Q[slot][:, 2 * parity + m, :], K[slot][:, 0, :]
                    elif kind == "swa":
                        q, k = Q[slot][:, 2 * pair + parity, :], K[slot][:, 0, :]
                    else:
                        q, k = Q[slot][:, parity, :], K[slot][:, parity, :]
                    n = P * len(keys)
                    for c in range(0, n, 512):
                        w = min(512, n - c)
                        nc.tensor.matmul(dst[:, c:c + w], q[:, P * tile:P * tile + P],
                                         k[:, P * keys[0] + c:P * keys[0] + c + w], start=True, stop=c + w < n)
                    if kind == "swa" and tile:
                        nc.tensor.matmul(dst[:, 0:P], ident_b[:, :], mask_prev[:, :], start=False, stop=False)
                    mm = nc.tensor.matmul(dst[:, n - P:n], ident_b[:, :],
                                          (mask_causal if kind == "fox" else mask_chunk)[:, :],
                                          start=False, stop=True)
                    mm.then_inc(wide_full, 1)

            def turn(s):
                _, kind, _, _, tile = STEPS[s]
                keys = key_tiles(kind, tile)
                pe.wait_ge(probs_ready, s + 1)
                parts = [keys[c:c + 4] for c in range(0, len(keys), 4)]
                for n, part in enumerate(parts):
                    c = chunk_of[s] + n
                    transposes(c, [(ptb[c % 2][:, P * b:P * b + P],
                                    probs[:, s % 2, 0, P * (4 * n + b):P * (4 * n + b) + P])
                                   for b in range(len(part))])

            def values(s):
                _, kind, pair, parity, tile = STEPS[s]
                keys = key_tiles(kind, tile)
                parts = [keys[c:c + 4] for c in range(0, len(keys), 4)]
                if s // 2 >= 2:
                    pe.wait_ge(o_read, s // 2 - 1)
                dst = (obank, sbank)[s // 2 % 2][64 * parity:64 * parity + 64, 0:P]
                vc = 64 * pair if kind == "swa" else P * pair + 64 * parity
                for n, part in enumerate(parts):
                    pe.wait_ge(pt_copied, chunk_of[s] + n + 1)
                    for b, kt in enumerate(part):
                        j = 4 * n + b
                        mm = nc.tensor.matmul(dst, VAL[kind][:, kt, vc:vc + 64], probsT[:, s % 2, j, :],
                                              start=(j == 0), stop=(j == len(keys) - 1))
                mm.then_inc(pv_done, 1)

            def cumulate():
                item = item_of["cum"]
                pe.wait_ge(fstat_ready, 1)
                pe.wait_ge(consts_ready, 5)
                pe.wait_ge(wide_read, item - 1)
                for half in range(2):
                    last = 4 * half + 3
                    for t in range(last + 1):
                        c0 = max(P * t, HALF * half)
                        n = HALF * (half + 1) - c0
                        src = tri_ones[:, 0:n] if P * t >= HALF * half else tri_ones[:, P:P + n]
                        mm = nc.tensor.matmul(wide[item % 2][:, c0:c0 + n], fstat[:, t, :], src,
                                              start=(t == 0), stop=(t == last))
                mm.then_inc(wide_full, 1)

            for kind, what in PLAN:
                if kind == "proj":
                    projection(what)
                elif kind == "cum":
                    cumulate()
                elif kind == "scores":
                    scores(what)
                elif kind == "turn":
                    turn(what)
                else:
                    values(what)

            pe.wait_ge(wide_read, ATT_ITEMS)
            pe.wait_ge(conv_done, 2 * CONV_K)
            for h in range(2):
                for n in range(4):
                    for c in range(2):
                        mm = nc.tensor.transpose(wide[h][:, 256 * n + P * c:256 * n + P * c + P],
                                                 zc[:, c, P * (4 * h + n):P * (4 * h + n) + P], ident[:, :])
                mm.then_inc(cln_full, 1)
            for h in range(2):
                pe.wait_ge(cln_xn, h + 1)
                for c in range(2):
                    for n in range(4):
                        mm = nc.tensor.transpose(wide[h][:, HALF * c + P * n:HALF * c + P * n + P],
                                                 cln_x[:, h, n, P * c:P * c + P], ident[:, :])
                mm.then_inc(cln_back, 1)
            for c in range(2):
                pe.wait_ge(sq_ready, c + 1)
                pe.wait_ge(cln_act, c + 1)
                for half in range(2):
                    mm = nc.tensor.matmul(wide[c][:, HALF * half:HALF * half + HALF], blk_ones,
                                          squares[:, c, HALF * half:HALF * half + HALF], start=True, stop=True)
                mm.then_inc(rms_full, 1)

            def output_projection(first, src, tile):
                n = first + tile
                if tile >= 2:
                    pe.wait_ge(mix_read, n - 1)
                for c in range(2):
                    for k in range(KD):
                        mm = nc.tensor.matmul(wide[tile % 2][:, HALF * c:HALF * c + HALF],
                                              src[:, k, P * tile:P * tile + P],
                                              big_w[:, k, HALF * c:HALF * c + HALF],
                                              start=(k == 0), stop=(k == KD - 1))
                mm.then_inc(mix_full, 1)

            pe.wait_ge(bigw_loaded, 16)
            pe.wait_ge(rms_root, 2)
            pe.wait_ge(rms_done, 2)
            for t in range(5):
                output_projection(0, yT, t)
            ln_transposes("1", 0, NT + 4)
            for t in range(5, NT):
                output_projection(0, yT, t)
            pe.wait_ge(mem_loaded, 32)
            for n in range(4):
                c = CH_MEM + n
                transposes(c, [(ptb[c % 2][:, 256 * a + P * m:256 * a + P * m + P],
                                mem_nat[:, m, P * (2 * n + a):P * (2 * n + a) + P])
                               for a in range(2) for m in range(2)])
            pe.wait_ge(pt_copied, CH_MEM + 4)
            pe.wait_ge(mix_read, NT)
            for n in range(8):
                w = weights(("m", n))
                item = IT_MEM + n // 2
                if n % 2 == 0:
                    pe.wait_ge(wide_read, item - 1)
                for a in range(2):
                    dst = wide[item % 2][:, HALF * (n % 2) + 256 * a:HALF * (n % 2) + 256 * a + 256]
                    for k in range(KD):
                        lhs, rhs = (w[:, k, P * a:P * a + P], memT[:, k, :]) if n < 4 \
                            else (memT[:, k, P * a:P * a + P], w[:, k, :])
                        mm = nc.tensor.matmul(dst, lhs, rhs, start=(k == 0), stop=(k == KD - 1))
                if n % 2:
                    mm.then_inc(wide_full, 1)
            ln_transposes("1", 1, NT + 8)
            pe.wait_ge(pt_copied, CH_LN["1", 1] + KD)
            for n in range(8):
                w = weights(("xq", n))
                pe.wait_ge(wide_read, IT_XQ + n - 1)
                transposed_projection(wide[(IT_XQ + n) % 2], w, P * (n % 2)).then_inc(wide_full, 1)

            def x_scores(u):
                head, half = u // 2, u % 2
                item = x_item[("xs", u)]
                pe.wait_ge(wide_read, max(item - 1, IT_XQ + 8))
                for n in range(4):
                    for k in range(2):
                        mm = nc.tensor.matmul(wide[item % 2][:, 256 * n:256 * n + 256],
                                              qxT[:, 2 * head + k, P * (4 * half + n):P * (4 * half + n) + P],
                                              kmT[:, 2 * head + k, :], start=(k == 0), stop=(k == 1))
                mm.then_inc(wide_full, 1)

            def x_values(u):
                head = u // 2
                item = x_item[("xo", u)]
                pe.wait_ge(xprobs_ready, u + 1)
                for m in range(2):
                    c = CH_X + 2 * u + m
                    transposes(c, [(ptb[c % 2][:, P * n:P * n + P], xprobs[:, u % 2, n, P * m:P * m + P])
                                   for n in range(4)])
                pe.wait_ge(pt_copied, CH_X + 2 * u + 2)
                pe.wait_ge(wide_read, item - 1)
                for a in range(2):
                    for m in range(2):
                        c = 256 * head + P * a
                        mm = nc.tensor.matmul(wide[item % 2][:, HALF * a:HALF * a + HALF], vm[:, m, c:c + P],
                                              xprobsT[:, u % 2, m, :], start=(m == 0), stop=(m == 1))
                mm.then_inc(wide_full, 1)

            for what, u in X_ORDER:
                (x_scores if what == "xs" else x_values)(u)
            pe.wait_ge(bigw_loaded, 32)
            pe.wait_ge(wide_read, IT_X + 16)
            for t in range(5):
                output_projection(NT, yT, t)
            ln_transposes("2", 0, 2 * NT + 4)
            for t in range(5, NT):
                output_projection(NT, yT, t)
            ln_transposes("2", 1, 2 * NT + 8)

            pe.wait_ge(pt_copied, CH_LN["2", 1] + KD)
            pe.wait_ge(mix_read, 2 * NT)
            pe.wait_ge(rw_loaded, 32)
            transposed_projection(wide[IT_ROUTE % 2], rw, 0, N_EXP).then_inc(wide_full, 1)
            for n in range(4):
                what = ("sg", "su")[n % 2], n // 2
                w = weights(what)
                pe.wait_ge(wide_read, IT_SH + n - 1)
                transposed_projection(wide[(IT_SH + n) % 2], w, P * what[1]).then_inc(wide_full, 1)
                if n == 0:
                    pe.wait_ge(wide_read, IT_ROUTE + 1)
                    c = CH_ROUTE
                    transposes(c, [(ptb[c % 2][:, N_EXP * t:N_EXP * t + N_EXP], logitsT[:, P * t:P * t + P])
                                   for t in range(NT)])
            last = len(w_loads) - 1
            pe.wait_ge(w_loaded[last % N_W], w_count[last])
            wd_sh = w_ring[:, last % N_W, 0:2 * D].rearrange("p (k c) -> p k c", k=2)
            pe.wait_ge(hs_ready, 2)
            pe.wait_ge(wide_read, IT_SH + 4)
            for t in range(NT):
                if t >= 2:
                    pe.wait_ge(mix_read, 2 * NT + t - 1)
                for c in range(2):
                    for k in range(2):
                        mm = nc.tensor.matmul(wide[t % 2][:, HALF * c:HALF * c + HALF],
                                              hs[:, k, P * t:P * t + P], wd_sh[:, k, HALF * c:HALF * c + HALF],
                                              start=(k == 0), stop=(k == 1))
                mm.then_inc(mix_full, 1)

            pe.wait_ge(routed, 1)
            pe.wait_ge(consts_ready, 7)
            sel = rs_selb.rearrange("p t e -> p (t e)")
            nc.tensor.matmul(obank, tri_b[:, :], sel, start=True, stop=True).then_inc(rank_full, 1)
            nc.tensor.matmul(sbank, ones_b[:, :], sel, start=True, stop=True).then_inc(rank_full, 1)
            pe.wait_ge(blk_full, 1)
            nc.tensor.transpose(obank[0:1, 0:P], blk_exp[:, 0:1], ident[:, :]).then_inc(rank_full, 1)

            def frames_of_block(b, count, read):
                pe.wait_ge(onehot_ready, count)
                if read is not None:
                    pe.wait_ge(idx_ready, read)
                for t in range(NT):
                    mm = nc.tensor.matmul(sbank[:, 8 * b:8 * b + 6], onehot[:, b, t, :], slot_cols[:, b, t, :],
                                          start=(t == 0), stop=(t == NT - 1))
                mm.then_inc(idx_full, 1)

            def rows_transposed(b, landed, free):
                pe.wait_ge(gathered[b], landed)
                for n in range(2):
                    if free is not None:
                        pe.wait_ge(xt_copied, free + n)
                    for a in range(4):
                        k = 4 * n + a
                        mm = nc.tensor.transpose(ptb[n][:, P * a:P * a + P], xg[:, b, P * k:P * k + P],
                                                 ident[:, :])
                    mm.then_inc(xt_full, 1)

            pe.wait_ge(table_ready, 1)
            pe.wait_ge(pt_copied, CH_MOE)
            pe.wait_ge(mix_read, 3 * NT)
            for j in range(2):
                frames_of_block(j, j + 1, j or None)
            rows_transposed(0, 16, None)
            turns = pe.value_load(table[0:1, P:P + 1], min_val=1, max_val=MAX_TURNS)
            with pe.Fori(0, turns) as i:
                for b in range(2):
                    pe.wait_ge(xt_copied, 4 * i + 2 * b + 2)
                    pe.wait_ge(gu_loaded[b], 32 * i + 32)
                    for k in range(KD):
                        mm = nc.tensor.matmul(wide[0][:, HALF * b:HALF * b + HALF], xgT[:, b, k, :],
                                              gu_w[b][:, k, :], start=(k == 0), stop=(k == KD - 1))
                    mm.then_inc(gu_full, 1)
                    frames_of_block(b, 2 * i + b + 3, 2 * i + b + 2)
                    rows_transposed(1 - b, 16 * i + 16 + 16 * b, 4 * i + 2 * b + 1)
                    pe.wait_ge(h_ready, 2 * i + b + 1)
                    for k in range(2):
                        mm = nc.tensor.transpose(obank[:, 256 * b + P * k:256 * b + P * k + P],
                                                 h_exp[:, b, P * k:P * k + P], ident[:, :])
                    mm.then_inc(ht_full, 1)
                    pe.wait_ge(ht_copied, 2 * i + b + 1)
                    pe.wait_ge(wd_loaded[b], 16 * i + 16)
                    pe.wait_ge(y_ready, 2 * i + b + 1)
                    for c in range(2):
                        for k in range(2):
                            mm = nc.tensor.matmul(wide[1][:, HALF * c:HALF * c + HALF], hT_exp[:, b, k, :],
                                                  wd_w[b][:, k, HALF * c:HALF * c + HALF],
                                                  start=(k == 0), stop=(k == 1))
                    mm.then_inc(y_full, 1)

        @block.scalar
        def _(act):
            def chunk_full(c):
                act.wait_ge(pt_full, c + 1)

            chunk_full(0)
            nc.scalar.copy(cols[:, :], ptb[0][:, 0:N_ROWS]).then_inc(pt_copied, 1)

            def ln_root(ln, t):
                act.wait_ge(ln_stat, NT * ln + t + 1)
                nc.scalar.activation(rstd[:, t:t + 1], mv[:, t, 1:2], ACT.Sqrt, bias=LN_EPS).then_inc(ln_std, 1)

            def ln_copy(which, half, k):
                c = CH_LN[which, half] + k
                r = R_LN[which]
                chunk_full(c)
                nc.scalar.activation(hT[:, k, HALF * half:HALF * half + HALF], ptb[c % 2], ACT.Identity,
                                     bias=cols[:, r[1] + k:r[1] + k + 1],
                                     scale=cols[:, r[0] + k:r[0] + k + 1]).then_inc(pt_copied, 1)

            act.wait_ge(pt_copied, 1)
            for t in range(4):
                ln_root(0, t)
            for k in range(KD):
                ln_copy("in", 0, k)
                if k % 2:
                    ln_root(0, 4 + k // 2)
            for k in range(KD):
                ln_copy("in", 1, k)

            def item_full(item):
                act.wait_ge(wide_full, item + 1)

            def augment(pair, slot):
                for p in range(2):
                    row, at0 = 32 * (2 * pair + p), (64, 0)[p]
                    nc.scalar.copy(Q[slot][at0:at0 + 1, p, :], cumT[row:row + 1, :])
                    last = nc.scalar.mul(K[slot][at0 + 32:at0 + 33, p, :], cumT[row:row + 1, :], -1.0)
                last.then_inc(aug_ready, 1)

            def projected(what):
                item = item_of[what]
                item_full(item)
                src = wide[item % 2]
                kind, n = what[0], what[1]
                group = {0: 0, 1: 1, 2: 2, 3: 2, 4: 3, 5: 4}[n]
                slot = SLOT_OF[group]
                if kind == "a":
                    last = nc.scalar.copy(z[:, n, PAD:PAD + S], src)
                elif kind == "g":
                    last = nc.scalar.activation(sig[:, n, :], src, ACT.Sigmoid)
                elif kind == "q":
                    act.wait_ge(q_zeroed, Q_ZEROED[group])
                    if group < 2:
                        for m in range(4):
                            last = nc.scalar.mul(Q[slot][32 * m:32 * m + 32, m, :], src[32 * m:32 * m + 32, :],
                                                 32 ** -0.5)
                    else:
                        for p in range(2):
                            m = p if group > 2 else (n - 2) + 2 * p
                            last = nc.scalar.mul(Q[slot][64 * p:64 * p + 64, m, :], src[64 * p:64 * p + 64, :],
                                                 0.125)
                elif kind == "k" and group > 2:
                    for p in range(2):
                        last = nc.scalar.copy(K[slot][64 * p:64 * p + 64, p, :], src[64 * p:64 * p + 64, :])
                elif kind == "k":
                    last = nc.scalar.copy(K[slot][:, 0, :], src)
                elif n == 0:
                    last = nc.scalar.copy(V[0][:, 4 * what[2]:4 * what[2] + 4, :],
                                          src.rearrange("p (t c) -> p t c", t=4))
                elif n == 2:
                    last = nc.scalar.copy(V[1][:, :, 0:P], src.rearrange("p (t c) -> p t c", t=NT))
                else:
                    two = src.rearrange("p (t c) -> p t c", t=2)
                    t = 2 * what[2]
                    act.wait_ge(pv_done, DIFF_STEPS)
                    nc.scalar.copy(logf[:, 0, t:t + 2, :], two[:, :, 256:260])
                    last = nc.scalar.copy(V[0][:, t:t + 2, :], two[:, :, 0:256])
                last.then_inc(wide_read, 1)
                if what == ("k", 5):
                    augment(1, 0)

            def exponentials(s):
                group, kind, pair, parity, tile = STEPS[s]
                n = P * len(key_tiles(kind, tile))
                if s == 0:
                    act.wait_ge(glu_done, 2)
                if s >= 2:
                    act.wait_ge(pt_full, chunk_of[s - 1])
                for m in range(2 if kind == "diff" else 1):
                    item = item_of[("s", s, m)]
                    act.wait_ge(row_max, RMS_OF[(s, m)] + 1)
                    bias = negm[:, s % 2, m:m + 1]
                    if kind == "swa":
                        h = 2 * pair + parity
                        nc.scalar.activation(sums[:, s % 2, 1:2], sink[:, h:h + 1], ACT.Exp, bias=bias)
                    nc.scalar.activation(probs[:, s % 2, m, 0:n], wide[item % 2][:, 0:n], ACT.Exp, bias=bias,
                                         accum_out=sums[:, s % 2, m:m + 1]).then_inc(wide_read, 1)
                if s == FOX_LOG_AT:
                    act.wait_ge(fox_z, 1)
                    nc.scalar.activation(logf[:, 1], logf[:, 1], ACT.Exp).then_inc(fox_e, 1)
                    act.wait_ge(fox_e, 1)
                    nc.scalar.activation(logf[:, 1], logf[:, 1], ACT.Ln, bias=1.0).then_inc(fox_l, 1)

            def transposed(s):
                kind, tile = STEPS[s][1], STEPS[s][4]
                keys = key_tiles(kind, tile)
                if s == 0:
                    for n in range(2):
                        act.wait_ge(res_stored[n], 64)
                if s >= 2:
                    act.wait_ge(pv_done, s - 1)
                for n in range((len(keys) + 3) // 4):
                    c, b = chunk_of[s] + n, min(4, len(keys) - 4 * n)
                    chunk_full(c)
                    nc.scalar.copy(probsT[:, s % 2, 4 * n:4 * n + b, :],
                                   ptb[c % 2][:, 0:P * b].rearrange("p (k q) -> p k q", k=b)
                                   ).then_inc(pt_copied, 1)

            act.wait_ge(lam_sum, 1)
            nc.scalar.activation(lam[:, 2:4], lam[:, 0:2], ACT.Exp).then_inc(lam_exp, 1)
            for kind, what in PLAN:
                if kind == "proj":
                    projected(what)
                elif kind == "cum":
                    item_full(item_of[what])
                    nc.scalar.copy(cumT, wide[item_of[what] % 2]).then_inc(wide_read, 1)
                    act.wait_ge(wide_read, item_of[what] + 1)
                    augment(0, 1)
                elif kind == "scores":
                    exponentials(what)
                elif kind == "turn":
                    transposed(what)

            act.wait_ge(o_read, NS // 2)
            for c in range(2):
                nc.scalar.activation(squares[:, c, :], yT[:, c, :], ACT.Square).then_inc(sq_ready, 1)
            for h in range(2):
                act.wait_ge(cln_stat, 4 * h + 4)
                nc.scalar.activation(rstd[:, 4 * h:4 * h + 4], mv[:, 4 * h:4 * h + 4, 1], ACT.Sqrt,
                                     bias=LN_EPS).then_inc(cln_std, 1)
            for h in range(2):
                act.wait_ge(cln_back, h + 1)
                for c in range(2):
                    last = nc.scalar.activation(yT[:, 2 + c, HALF * h:HALF * h + HALF],
                                                wide[h][:, HALF * c:HALF * c + HALF], ACT.Silu,
                                                bias=cols[:, R_CLNB + c:R_CLNB + c + 1],
                                                scale=cols[:, R_CLNG + c:R_CLNG + c + 1])
                last.then_inc(cln_act, 1)
            for c in range(2):
                act.wait_ge(rms_full, c + 1)
                nc.scalar.activation(root[:, c, :], wide[c], ACT.Sqrt, bias=LN_EPS).then_inc(rms_root, 1)
            for t in range(5):
                ln_root(1, t)
            for k in range(KD):
                ln_copy("1", 0, k)
            for t in range(5, NT):
                ln_root(1, t)
            for n in range(4):
                c = CH_MEM + n
                chunk_full(c)
                nc.scalar.copy(memT[:, 2 * n:2 * n + 2, :], ptb[c % 2].rearrange("p (k m) -> p k m", k=2)
                               ).then_inc(pt_copied, 1)
            for n in range(4):
                item_full(IT_MEM + n)
                src = wide[(IT_MEM + n) % 2]
                if n < 2:
                    last = nc.scalar.copy(kmT[:, 4 * n:4 * n + 4, :], src.rearrange("p (k m) -> p k m", k=4))
                else:
                    four = src.rearrange("p (r a c) -> p r a c", r=2, a=2)
                    for a in range(2):
                        last = nc.scalar.copy(vm[:, a, HALF * (n - 2):HALF * (n - 1)]
                                              .rearrange("p (r c) -> p r c", r=2), four[:, :, a, :])
                last.then_inc(wide_read, 1)
            for k in range(KD):
                ln_copy("1", 1, k)
            act.wait_ge(res_ready, 2 * NT)
            for n in range(8):
                item_full(IT_XQ + n)
                nc.scalar.mul(qxT[:, n, :], wide[(IT_XQ + n) % 2], 1.0 / 16).then_inc(wide_read, 1)
            for what, u in X_ORDER:
                item = x_item[(what, u)]
                src = wide[item % 2]
                if what == "xs":
                    act.wait_ge(xmax, u + 1)
                    if u >= 2:
                        act.wait_ge(pt_full, CH_X + 2 * u - 2)
                    for n in range(4):
                        last = nc.scalar.activation(xprobs[:, u % 2, n, :], src[:, 256 * n:256 * n + 256], ACT.Exp,
                                                    bias=xneg[:, u % 2, n:n + 1],
                                                    accum_out=xsum[:, u % 2, n:n + 1])
                    last.then_inc(wide_read, 1)
                else:
                    if u == 0:
                        for n in range(2):
                            act.wait_ge(res_stored[n], 128)
                    for m in range(2):
                        c = CH_X + 2 * u + m
                        chunk_full(c)
                        nc.scalar.copy(xprobsT[:, u % 2, m, :], ptb[c % 2]).then_inc(pt_copied, 1)
                    item_full(item)
                    k, half = 2 * (u // 2), u % 2
                    nc.scalar.copy(yT[:, k:k + 2, HALF * half:HALF * half + HALF],
                                   src.rearrange("p (a s) -> p a s", a=2)).then_inc(wide_read, 1)
            for t in range(5):
                ln_root(2, t)
            for k in range(KD):
                ln_copy("2", 0, k)
            for t in range(5, NT):
                ln_root(2, t)
            for k in range(KD):
                ln_copy("2", 1, k)
            item_full(IT_ROUTE)
            nc.scalar.copy(logitsT, wide[IT_ROUTE % 2][0:N_EXP, :]).then_inc(wide_read, 1)
            chunk_full(CH_ROUTE)
            nc.scalar.activation(rs_scores, ptb[CH_ROUTE % 2].rearrange("p (t e) -> p t e", t=NT),
                                 ACT.Sigmoid).then_inc(pt_copied, 1)
            for m in range(2):
                item_full(IT_SH + 2 * m)
                nc.scalar.activation(hs[:, m, :], wide[(IT_SH + 2 * m) % 2], ACT.Silu).then_inc(wide_read, 1)
                item_full(IT_SH + 2 * m + 1)
                if m:
                    act.wait_ge(hs_ready, 1)
                nc.scalar.copy(hs_tmp, wide[(IT_SH + 2 * m + 1) % 2]).then_inc(wide_read, 1)

            act.sem_inc(y_ready, 1)
            def copy_rows(b, n, full):
                act.wait_ge(xt_full, full)
                nc.scalar.copy(xgT[:, b, 4 * n:4 * n + 4, :],
                               ptb[n].rearrange("p (k r) -> p k r", k=4)).then_inc(xt_copied, 1)

            for n in range(2):
                copy_rows(0, n, n + 1)
            act.wait_ge(table_ready, 1)
            turns = act.value_load(table[0:1, P:P + 1], min_val=1, max_val=MAX_TURNS)
            with act.Fori(0, turns) as i:
                for b in range(2):
                    act.wait_ge(gu_full, 2 * i + b + 1)
                    nc.scalar.activation(h_exp[:, b, :], wide[0][:, HALF * b:HALF * b + D_EXP],
                                         ACT.Silu).then_inc(silu_done, 1)
                    for n in range(2):
                        copy_rows(1 - b, n, 4 * i + 2 * b + n + 3)
                    act.wait_ge(y_full, 2 * i + b + 1)
                    act.wait_ge(scattered, 32 * i + 16 * b + 16)
                    nc.scalar.copy(y_exp[:, b, :], wide[1]).then_inc(y_ready, 1)
            for t in range(NT):
                ln_root(3, t)

        @block.vector
        def _(dve):
            chain = [0]

            def link(made):
                chain[0] += 1
                made.then_inc(dve_step, 1)
                dve.wait_ge(dve_step, chain[0])

            def layer_norm_tiles(ln, tile_ready):
                x = xnorm["in" if ln == 0 else str(ln)]
                for t in range(NT + 1):
                    if t < NT:
                        tile_ready(t)
                        for h in range(2):
                            last = nc.vector.bn_stats(stats[:, t, h, :], x[:, t, HALF * h:HALF * h + HALF])
                        link(last)
                        nc.vector.bn_aggr(mv[:, t, :], stats[:, t, :, :]).then_inc(ln_stat, 1)
                    if t:
                        u = t - 1
                        dve.wait_ge(ln_std, NT * ln + u + 1)
                        link(nc.vector.reciprocal(rstd[:, u:u + 1], rstd[:, u:u + 1]))
                        nc.vector.tensor_scalar(x[:, u, :], x[:, u, :], mv[:, u, 0:1], rstd[:, u:u + 1],
                                                ALU.subtract, ALU.mult).then_inc(ln_done, 1)

            layer_norm_tiles(0, lambda t: dve.wait_ge(x_loaded[t], 16))
            dve.wait_ge(params_loaded, 96)
            for n in range(2):
                last = nc.vector.tensor_tensor_reduce(lamv[:, 2 * n, :], lamv[:, 2 * n, :], lamv[:, 2 * n + 1, :],
                                                      1.0, 0.0, ALU.mult, ALU.add, lam[:, n:n + 1])
            last.then_inc(lam_sum, 1)
            dve.wait_ge(lam_exp, 1)
            link(nc.vector.tensor_tensor(lam[:, 4:5], lam[:, 3:4], lam[:, 2:3], ALU.subtract))
            link(nc.vector.tensor_scalar(lam[:, 5:6], lam[:, 4:5], -LAMBDA_INIT, None, ALU.add))
            neg_lam = lam[:, 5:6]
            nc.vector.tensor_scalar(nsink[:, :], sink[:, :], -1.0, None, ALU.mult)
            dve.wait_ge(pt_copied, 1)
            link(nc.vector.tensor_scalar(subg[:, :], cols[:, R_SUBG:R_SUBG + 1], 1.0 - LAMBDA_INIT, None, ALU.mult))
            for c in range(2):
                link(nc.vector.memset(z[:, c, 0:PAD], 0.0))
                dve.wait_ge(wide_read, item_of[("g", c)] + 1)
                nc.vector.tensor_tensor(z[:, c, PAD:PAD + S], z[:, c, PAD:PAD + S], sig[:, c, :],
                                        ALU.mult).then_inc(glu_done, 1)

            def conv_tap(n):
                c, k = n // CONV_K, n % CONV_K
                w = cols[:, R_CONVW + n:R_CONVW + n + 1]
                if k == 0:
                    dve.wait_ge(glu_done, c + 1)
                    nc.vector.tensor_scalar(zc[:, c, :], z[:, c, 0:S], w, cols[:, R_CONVB + c:R_CONVB + c + 1],
                                            ALU.mult, ALU.add).then_inc(conv_done, 1)
                else:
                    dve.wait_ge(conv_done, n)
                    nc.vector.scalar_tensor_tensor(zc[:, c, :], z[:, c, k:k + S], w, zc[:, c, :],
                                                   ALU.mult, ALU.add).then_inc(conv_done, 1)

            def maxima(s):
                group, kind, pair, parity, tile = STEPS[s]
                n = P * len(key_tiles(kind, tile))
                for m in range(2 if kind == "diff" else 1):
                    item = item_of[("s", s, m)]
                    dve.wait_ge(wide_full, item + 1)
                    made = nc.vector.tensor_reduce(negm[:, s % 2, m:m + 1], wide[item % 2][:, 0:n], AX.X, ALU.max,
                                                   negate=True)
                    if kind == "swa":
                        h = 2 * pair + parity
                        link(made)
                        made = nc.vector.tensor_tensor(negm[:, s % 2, 0:1], negm[:, s % 2, 0:1],
                                                       nsink[:, h:h + 1], ALU.min)
                    made.then_inc(row_max, 1)

            def normalise(s):
                kind, tile = STEPS[s][1], STEPS[s][4]
                n = P * len(key_tiles(kind, tile))
                maps = 2 if kind == "diff" else 1
                p = probs[:, s % 2]
                r = rsum[:, s % 2]
                dve.wait_ge(wide_read, item_of[("s", s, maps - 1)] + 1)
                if kind == "diff":
                    link(nc.vector.reciprocal(r[:, 0:2], sums[:, s % 2, :]))
                    link(nc.vector.tensor_tensor(r[:, 2:3], r[:, 1:2], neg_lam, ALU.mult))
                    link(nc.vector.tensor_scalar(p[:, 1, 0:n], p[:, 1, 0:n], r[:, 2:3], None, ALU.mult))
                    nc.vector.scalar_tensor_tensor(p[:, 0, 0:n], p[:, 0, 0:n], r[:, 0:1], p[:, 1, 0:n],
                                                   ALU.mult, ALU.add).then_inc(probs_ready, 1)
                    return
                total = sums[:, s % 2, 0:1]
                if kind == "swa":
                    link(nc.vector.tensor_tensor(r[:, 1:2], sums[:, s % 2, 0:1], sums[:, s % 2, 1:2], ALU.add))
                    total = r[:, 1:2]
                link(nc.vector.reciprocal(r[:, 0:1], total))
                nc.vector.tensor_scalar(p[:, 0, 0:n], p[:, 0, 0:n], r[:, 0:1], None, ALU.mult).then_inc(probs_ready, 1)

            def output_read(pair_step):
                s = 2 * pair_step
                _, kind, pair, _, tile = STEPS[s]
                dve.wait_ge(pv_done, s + 2)
                nc.vector.tensor_copy(yT[:, Y_CHUNK[kind] + pair, P * tile:P * tile + P],
                                      (obank, sbank)[pair_step % 2][:, 0:P]).then_inc(o_read, 1)

            def fox_log():
                x = logf[:, 0]
                link(nc.vector.tensor_tensor(x, x, foxb[:, :].unsqueeze(1).broadcast_to([P, NT, 4]), ALU.add))
                nc.vector.scalar_tensor_tensor(logf[:, 1], x, -1.0, x, ALU.mult, ALU.min).then_inc(fox_z, 1)
                dve.wait_ge(res_ready, NT)
                link(nc.vector.memset(fstat, 0.0))

            def fox_log_end():
                dve.wait_ge(fox_l, 1)
                nc.vector.scalar_tensor_tensor(fstat[:, :, 0:P:32], logf[:, 0], 0.0, logf[:, 1],
                                               ALU.min, ALU.subtract).then_inc(fstat_ready, 1)

            for kind, what in PLAN:
                if kind == "scores":
                    if what == FOX_LOG_AT:
                        fox_log()
                    if what:
                        normalise(what - 1)
                    maxima(what)
                    if what == FOX_LOG_AT + 1:
                        fox_log_end()
                    if what < 2 * CONV_K:
                        conv_tap(what)
                elif kind == "turn" and what == NS - 1:
                    normalise(what)
                elif kind == "values":
                    if what % 2 == 0 and what >= 2:
                        output_read(what // 2 - 1)
            output_read(NS // 2 - 1)

            dve.wait_ge(pt_full, ATT_CHUNKS)
            link(nc.vector.memset(blk_ones, 0.0))
            for p in range(2):
                last = nc.vector.memset(blk_ones[64 * p:64 * p + 64, 64 * p:64 * p + 64], 1.0 / 64)
            link(last)
            for h in range(2):
                dve.wait_ge(cln_full, h + 1)
                for n in range(4):
                    last = nc.vector.bn_stats(stats[:, 4 * h + n, 0, :], wide[h][:, 256 * n:256 * n + 256])
                link(last)
                for n in range(4):
                    nc.vector.bn_aggr(mv[:, 4 * h + n, :], stats[:, 4 * h + n, 0, :]).then_inc(cln_stat, 1)
            for h in range(2):
                dve.wait_ge(cln_std, h + 1)
                link(nc.vector.reciprocal(rstd[:, 4 * h:4 * h + 4], rstd[:, 4 * h:4 * h + 4]))
                for n in range(4):
                    t = 4 * h + n
                    last = nc.vector.tensor_scalar(cln_x[:, h, n, :], wide[h][:, 256 * n:256 * n + 256],
                                                   mv[:, t, 0:1], rstd[:, t:t + 1], ALU.subtract, ALU.mult)
                last.then_inc(cln_xn, 1)
            for c in range(2):
                dve.wait_ge(rms_root, c + 1)
                link(nc.vector.reciprocal(root[:, c, :], root[:, c, :]))
                nc.vector.scalar_tensor_tensor(yT[:, c, :], yT[:, c, :], subg[:, 0:1], root[:, c, :],
                                               ALU.mult, ALU.mult).then_inc(rms_done, 1)

            def add_products(ln, first):
                def ready(t):
                    n = first + t
                    dve.wait_ge(x_loaded[t], 16 * (ln + 1))
                    dve.wait_ge(mix_full, n + 1)
                    x = xnorm[str(ln)][:, t, :]
                    nc.vector.tensor_tensor(x, x, wide[t % 2], ALU.add).then_inc(mix_read, 1)
                    dve.wait_ge(mix_read, n + 1)
                return ready

            layer_norm_tiles(1, add_products(1, 0))
            for u in range(8):
                item = x_item[("xs", u)]
                dve.wait_ge(wide_full, item + 1)
                nc.vector.tensor_reduce(xneg[:, u % 2, :], wide[item % 2].rearrange("p (t m) -> p t m", t=4), AX.X,
                                        ALU.max, negate=True).then_inc(xmax, 1)
                dve.wait_ge(wide_read, item + 1)
                link(nc.vector.reciprocal(xsum[:, u % 2, :], xsum[:, u % 2, :]))
                nc.vector.tensor_tensor(xprobs[:, u % 2], xprobs[:, u % 2],
                                        xsum[:, u % 2, :].unsqueeze(2).broadcast_to([P, 4, N_MEM]),
                                        ALU.mult).then_inc(xprobs_ready, 1)
            layer_norm_tiles(2, add_products(2, NT))

            def hidden(m):
                dve.wait_ge(wide_read, IT_SH + 2 * m + 2)
                nc.vector.tensor_tensor(hs[:, m, :], hs[:, m, :], hs_tmp, ALU.mult).then_inc(hs_ready, 1)

            dve.wait_ge(pt_copied, CH_ROUTE + 1)
            nc.vector.memset(rs_choice[:, :, N_EXP:N_EXP + 2], SENTINEL)
            nc.vector.memset(gsum[:, :, N_GRP:12], SENTINEL)
            link(nc.vector.tensor_tensor(rs_choice[:, :, 0:N_EXP], rs_scores,
                                         rbias.unsqueeze(1).broadcast_to([P, NT, N_EXP]), ALU.add))
            for t in range(NT):
                for g in range(N_GRP):
                    last = nc.vector.max(top8[:, t, g, :], rs_choice[:, t, PER_GRP * g:PER_GRP * g + PER_GRP])
            link(last)
            link(nc.vector.tensor_tensor(gsum[:, :, 0:N_GRP], top8[:, :, :, 0], top8[:, :, :, 1], ALU.add))

            def take_top(n_take, values, n_values, n_padded, largest):
                for t in range(NT):
                    last = nc.vector.max(largest[:, t, :], values[:, t, 0:n_values])
                link(last)
                link(nc.vector.memset(largest[:, :, n_take:8], SENTINEL))
                for t in range(NT):
                    last = nc.vector.match_replace(values[:, t, 0:n_padded], largest[:, t, :],
                                                   values[:, t, 0:n_padded], TAKEN)
                link(last)

            take_top(TOP_GRP, gsum, N_GRP, 12, gtop)
            link(nc.vector.tensor_scalar(gpen[:, :, 0:N_GRP], gsum[:, :, 0:N_GRP], TAKEN / 3, NEG, ALU.is_lt, ALU.mult))
            by_group = rs_choice[:, :, 0:N_EXP].rearrange("p t (g e) -> p t g e", g=N_GRP)
            for t in range(NT):
                last = nc.vector.tensor_tensor(by_group[:, t], by_group[:, t],
                                               gpen[:, t, 0:N_GRP].unsqueeze(2).broadcast_to([P, N_GRP, PER_GRP]),
                                               ALU.add)
            link(last)
            take_top(TOP_K, rs_choice, N_EXP, N_EXP + 2, gtop)
            link(nc.vector.tensor_scalar(rs_sel, rs_choice[:, :, 0:N_EXP], TAKEN / 3, None, ALU.is_gt))
            nc.vector.tensor_copy(rs_selb, rs_sel).then_inc(routed, 1)
            hidden(0)
            link(nc.vector.tensor_tensor(rs_gate, rs_sel, rs_scores, ALU.mult))
            link(nc.vector.tensor_reduce(gden[:, :, 0], rs_gate, AX.X, ALU.add))
            link(nc.vector.reciprocal(gden[:, :, 1], gden[:, :, 0]))
            link(nc.vector.tensor_tensor(rs_gate, rs_gate, gden[:, :, 1].unsqueeze(2).broadcast_to([P, NT, N_EXP]),
                                         ALU.mult))
            link(nc.vector.tensor_scalar(rs_gate, rs_gate, ROUTED_SCALE, None, ALU.mult))
            for g in range(3):
                part = gparts[:, :, :, g].rearrange("p e t -> p t e")
                link(nc.vector.tensor_copy(part, rs_gate))
                if g < 2:
                    link(nc.vector.tensor_tensor(rs_gate, rs_gate, part, ALU.subtract))
            hidden(1)
            dve.wait_ge(h_stored, 16 * NT)
            for t in range(NT):
                dve.wait_ge(mix_full, 2 * NT + t + 1)
                x = xnorm["2"][:, t, :]
                nc.vector.scalar_tensor_tensor(x, x, ALPHA, wide[t % 2], ALU.mult, ALU.add).then_inc(mix_read, 1)
            dve.wait_ge(rank_full, 2)
            counts = sbank.rearrange("p (t e) -> p t e", t=NT)
            link(nc.vector.memset(rs_off[:, 0, :], 0.0))
            for t in range(NT):
                link(nc.vector.tensor_tensor(rs_off[:, t + 1, :], rs_off[:, t, :], counts[:, t, :], ALU.add))
            link(nc.vector.tensor_tensor(rs_rank, rs_off[:, 0:NT, :], obank.rearrange("p (t e) -> p t e", t=NT),
                                         ALU.add))
            link(nc.vector.tensor_scalar(nb_i[:, :], rs_off[:, NT, :], float(EXP_BLOCK - 1), None, ALU.add))
            link(nc.vector.tensor_scalar(nb_i[:, :], nb_i[:, :], 7, None, ALU.logical_shift_right))
            link(nc.vector.tensor_copy(nb_f[:, 0, :], nb_i[:, :]))
            link(nc.vector.tensor_copy(nb_f[:, 1, :], nb_f[:, 0, :]))
            src, k = 1, 1
            while k < N_EXP:
                dst = 3 - src
                nc.vector.tensor_copy(nb_f[:, dst, 0:k], nb_f[:, src, 0:k])
                link(nc.vector.tensor_tensor(nb_f[:, dst, k:], nb_f[:, src, k:], nb_f[:, src, 0:N_EXP - k], ALU.add))
                src, k = dst, 2 * k
            ends = nb_f[:, src, :]
            starts = nb_f[:, 0, :]
            tmp = nb_f[:, 3 - src, :]
            link(nc.vector.tensor_scalar(tmp, ends, pcol[:, 0:1], None, ALU.is_le))
            link(nc.vector.tensor_reduce(blk_exp[:, 0:1], tmp, AX.X, ALU.add))
            nc.vector.tensor_scalar(blk_exp[:, 0:1], blk_exp[:, 0:1], float(N_EXP - 1), None,
                                    ALU.min).then_inc(blk_full, 1)
            link(nc.vector.tensor_scalar(table[0:1, P:P + 1], ends[0:1, N_EXP - 1:N_EXP], 1.0, None, ALU.add))
            link(nc.vector.tensor_scalar(table[0:1, P:P + 1], table[0:1, P:P + 1], 1, None, ALU.logical_shift_right))
            link(nc.vector.tensor_tensor(starts, ends, starts, ALU.subtract))
            link(nc.vector.tensor_scalar(starts, starts, float(EXP_BLOCK), 1.0, ALU.mult, ALU.add))
            link(nc.vector.tensor_tensor(rs_rank, rs_rank, starts.unsqueeze(1).broadcast_to([P, NT, N_EXP]), ALU.add))
            link(nc.vector.tensor_tensor(rs_rank, rs_rank, rs_sel, ALU.mult))
            link(nc.vector.tensor_scalar(dest.rearrange("p e t -> p t e"), rs_rank, -1.0, None, ALU.add))
            nc.vector.memset(y_exp[:, 0, :], 0.0).then_inc(moe_setup, 1)
            link(nc.vector.memset(blk_base[:, :], 0.0))
            dve.wait_ge(rank_full, 3)
            nc.vector.tensor_copy(table[0:1, 0:P], obank[0:1, 0:P]).then_inc(table_ready, 1)
            dve.wait_ge(table_ready, 1)

            LINKS = 4
            at_link = [0]

            def step(made, i):
                at_link[0] += 1
                made.then_inc(moe_step, 1)
                dve.wait_ge(moe_step, at_link[0] if i is None else 2 * LINKS * i + at_link[0])

            def one_hot(b, e, i):
                step(nc.vector.tensor_scalar(d8[:, :].unsqueeze(1), dest[:, bass.ds(e, 1), :], blk_base[:, 0:1], None,
                                             ALU.subtract), i)
                nc.vector.tensor_copy(slot_cols[:, b, :, 3:6],
                                      gparts[:, bass.ds(e, 1), :, :].rearrange("p o t g -> p (o t) g"))
                step(nc.vector.tensor_scalar(blk_base[:, :], blk_base[:, :], float(EXP_BLOCK), None, ALU.add), i)
                nc.vector.tensor_tensor(onehot[:, b], iota_s[:, :].unsqueeze(1).broadcast_to([P, NT, P]),
                                        d8[:, :].unsqueeze(2).broadcast_to([P, NT, P]),
                                        ALU.is_equal).then_inc(onehot_ready, 1)

            def frames(b, i):
                got = sbank[:, 8 * b:8 * b + 8]
                nc.vector.tensor_reduce(idx_tmp[:, b, 0:1], got[:, 0:2], AX.X, ALU.add)
                nc.vector.tensor_scalar(idx_tmp[:, b, 1:2], got[:, 2:3], pcol[:, 1:2], pcol[:, 2:3],
                                        ALU.mult, ALU.add)
                step(nc.vector.tensor_reduce(gate_new[:, b:b + 1], got[:, 3:6], AX.X, ALU.add), i)
                nc.vector.tensor_tensor(idx_new[:, b:b + 1], idx_tmp[:, b, 0:1], idx_tmp[:, b, 1:2],
                                        ALU.add).then_inc(idx_ready, 1)

            for j in range(3):
                e = dve.value_load(table[0:1, j:j + 1], min_val=0, max_val=N_EXP - 1)
                if j == 2:
                    dve.wait_ge(idx_full, 1)
                one_hot(j % 2, e, None)
                if j < 2:
                    dve.wait_ge(idx_full, j + 1)
                    frames(j, None)
            turns = dve.value_load(table[0:1, P:P + 1], min_val=1, max_val=MAX_TURNS)
            with dve.Fori(0, turns) as i:
                for b in range(2):
                    dve.wait_ge(idx_ready, 2 * i + b + 1)
                    dve.wait_ge(scattered, 32 * i + 16 * b + 16)
                    nc.vector.tensor_copy(idx_now[:, b:b + 1], idx_new[:, b:b + 1])
                    step(nc.vector.tensor_copy(gate_now[:, b:b + 1], gate_new[:, b:b + 1]), i)
                    e = dve.value_load(table[0:1, bass.ds(2 * i + 3 + b, 1)], min_val=0, max_val=N_EXP - 1)
                    dve.wait_ge(idx_full, 2 * i + b + 2)
                    one_hot(1 - b, e, i)
                    dve.wait_ge(silu_done, 2 * i + b + 1)
                    nc.vector.scalar_tensor_tensor(h_exp[:, b, :], h_exp[:, b, :], gate_now[:, b:b + 1],
                                                   wide[0][:, HALF * b + D_EXP:HALF * b + 2 * D_EXP],
                                                   ALU.mult, ALU.mult).then_inc(h_ready, 1)
                    dve.wait_ge(ht_full, 2 * i + b + 1)
                    nc.vector.tensor_copy(hT_exp[:, b], obank[:, 256 * b:256 * b + 256]
                                          .rearrange("p (k r) -> p k r", k=2)).then_inc(ht_copied, 1)
                    dve.wait_ge(idx_full, 2 * i + b + 3)
                    frames(b, i)
            layer_norm_tiles(3, lambda t: dve.wait_ge(x_loaded[t], 64))


def kernel(**inputs):
    import numpy as _np
    import concourse.bacc as _bacc
    from concourse.bass_utils import run_bass_kernel_spmd as _run

    nc = _bacc.Bacc("TRN2", target_bir_lowering=False, num_devices=1)
    arrays, ins = {}, {}
    for name, value in inputs.items():
        a = _np.ascontiguousarray(value)
        arrays[f"in_{name}"] = a
        ins[name] = nc.dram_tensor(f"in_{name}", a.shape, mybir.dt.from_np(a.dtype), kind="ExternalInput").ap()
    out = nc.dram_tensor("out_h", (1, S, D), F32, kind="ExternalOutput").ap()
    h_res = nc.dram_tensor("h_res", (S, D), F32, kind="Internal").ap()
    h_table = nc.dram_tensor("h_table", (S + P, D), F32, kind="Internal").ap()
    acc = nc.dram_tensor("acc", (S + P, D), F32, kind="Internal").ap()
    build(nc, ins, out, h_res, h_table, acc)
    r = _run(nc, [arrays], core_ids=[0])
    return r.results[0]["out_h"]
```

```python
from contextlib import ExitStack

import concourse.bass as bass
from concourse import mybir

F32 = mybir.dt.float32
F32R = mybir.dt.float32r
BF16 = mybir.dt.bfloat16
I32 = mybir.dt.int32
ACT = mybir.ActivationFunctionType
ALU = mybir.AluOpType
AX = mybir.AxisListType

P = 128
S = 1024
D = 1024
NT = S // P
KD = D // P
HALF = 512
CHUNK = 64
N_MEM = 256
CONV_K = 31
PAD = CONV_K - 1
X_HEADS = 4
N_EXP = 64
N_GRP = 8
PER_GRP = N_EXP // N_GRP
TOP_GRP = 4
TOP_K = 6
D_EXP = 256
EXP_BLOCK = 128
MAX_BLOCKS = (S * TOP_K) // EXP_BLOCK + N_EXP
LN_EPS = 1e-5
ALPHA = 2.0 ** 0.25
LAMBDA_INIT = 0.2
ROUTED_SCALE = 2.5
NEG = -1e30
SENTINEL = -3e38
TAKEN = 3e38

C_AQ, C_AK, C_AV, C_CU = 0, 256, 512, 768
C_SQ, C_SK, C_SV = 1280, 1536, 1664
C_FQ, C_FK, C_FV, C_FF = 1792, 2048, 2304, 2560
N_IN = 2564

R_LN = {"in": (0, 8), "1": (16, 24), "2": (32, 40)}
R_CONVB, R_CLNG, R_CLNB, R_SUBG, R_CONVW = 48, 50, 52, 54, 55
N_ROWS = R_CONVW + 2 * CONV_K

DIFF_STEPS = 2 * NT * 2
AUGMENT_AT = (DIFF_STEPS + 22, DIFF_STEPS + 42)
FOX_LOG_AT = DIFF_STEPS + 14
U = 1024


def attention_steps():
    steps = []
    for group, kind, pairs in ((0, "diff", [0]), (1, "diff", [1]), (2, "swa", [0, 1]),
                               (3, "fox", [0]), (4, "fox", [1])):
        for pair in pairs:
            for tile in range(NT):
                for parity in range(2):
                    steps.append((group, kind, pair, parity, tile))
    return steps


def key_tiles(kind, tile):
    return list(range(max(0, tile - 1), tile + 1)) if kind == "swa" else list(range(tile + 1))


def make_plan():
    steps = attention_steps()
    proj = {
        0: [("q", 0), ("k", 0), ("v", 0, 0), ("v", 0, 1)],
        1: [("q", 1), ("k", 1)],
        2: [("q", 2), ("q", 3), ("k", 2), ("v", 2, 0)],
        3: [("q", 4), ("k", 4), ("v", 4, 0), ("v", 4, 1), ("v", 4, 2), ("v", 4, 3)],
        4: [("q", 5), ("k", 5)],
    }
    plan = [("proj", ("a", 0)), ("proj", ("g", 0)), ("proj", ("a", 1)), ("proj", ("g", 1))]
    plan += [("proj", p) for p in proj[0] + proj[1]]
    starts = {g: next(n for n, step in enumerate(steps) if step[0] == g) for g in range(5)}
    at = {}
    for g in range(2, 5):
        for n, p in enumerate(proj[g]):
            at[starts[g - 1] + 2 + (2 if len(proj[g]) > 2 else 5) * n] = ("proj", p)
    at[FOX_LOG_AT + 3] = ("cum", "cum")
    for s in range(len(steps) + 2):
        if s in at:
            plan.append(at[s])
        if s >= 2:
            plan.append(("turn", s - 2))
        if s < len(steps):
            plan.append(("scores", s))
        if s >= 2:
            plan.append(("values", s - 2))
    return steps, plan


def build(nc, ins, out, h_res, h_table, acc):
    STEPS, PLAN = make_plan()
    NS = len(STEPS)
    item_of, n_items = {}, 0
    for kind, what in PLAN:
        if kind in ("proj", "cum"):
            item_of[what] = n_items
            n_items += 1
        elif kind == "scores":
            for m in range(2 if STEPS[what][1] == "diff" else 1):
                item_of[("s", what, m)] = n_items
                n_items += 1
    ATT_ITEMS = n_items
    GROUP_READY = {0: item_of[("v", 0, 1)], 1: item_of[("k", 1)], 2: item_of[("v", 2, 0)],
                   3: item_of[("v", 4, 3)], 4: item_of[("k", 5)]}
    LN_CHUNKS = 2 * KD
    chunk_of, n_chunks = {}, 1 + LN_CHUNKS
    for s, (_, kind, _, _, tile) in enumerate(STEPS):
        nk = len(key_tiles(kind, tile))
        chunk_of[s] = n_chunks
        n_chunks += (nk + 3) // 4
    ATT_CHUNKS = n_chunks
    CH_LN = {("in", 0): 1, ("in", 1): 1 + KD, ("1", 0): ATT_CHUNKS}
    CH_MEM = ATT_CHUNKS + KD
    CH_LN["1", 1] = CH_MEM + 4
    CH_X = CH_LN["1", 1] + KD
    CH_LN["2", 0] = CH_X + 16
    CH_LN["2", 1] = CH_LN["2", 0] + KD
    CH_ROUTE = CH_LN["2", 1] + KD
    CH_MOE = CH_ROUTE + 1
    IT_MEM = ATT_ITEMS
    IT_XQ = IT_MEM + 4
    IT_X = IT_XQ + 8
    X_ORDER = [("xs", 0)]
    for u in range(8):
        if u + 1 < 8:
            X_ORDER.append(("xs", u + 1))
        X_ORDER.append(("xo", u))
    x_item = {w: IT_X + n for n, w in enumerate(X_ORDER)}
    IT_ROUTE = IT_X + 16
    IT_SH = IT_ROUTE + 1

    with ExitStack() as ctx:
        def sb(name, shape, dt=F32):
            return ctx.enter_context(nc.sbuf_tensor(name, shape, dt))

        def sem(name):
            return ctx.enter_context(nc.semaphore(name))

        W_SLOT = KD * 260
        N_W = 3
        arena_at = -(-nc.sbuf_base // 32) * 32
        arena = sb("arena", [P, 42 * U + 64 + 640 + N_W * W_SLOT])
        at = [0]

        def cut(n):
            a = arena[:, at[0]:at[0] + n]
            at[0] += n
            return a

        def placed(name, first, *shape, dt=F32R):
            return nc.alloc_sbuf_tensor_at(name, [P, *shape], dt, offset=arena_at + 4 * first)

        hT = cut(8 * U).rearrange("p (k s) -> p k s", k=KD)
        yT_flat = cut(8 * U)
        yT = yT_flat.rearrange("p (k s) -> p k s", k=KD)
        qkv0 = cut(8 * U)
        qkv1 = cut(8 * U)
        probs_flat = cut(4 * U)
        pT_flat = cut(2 * U)
        conv_flat = cut(4 * U + 64)
        misc = cut(640)
        w_ring = cut(N_W * W_SLOT).rearrange("p (n c) -> p n c", n=N_W)
        gb = sb("gb", [P, 2 * U])

        Q = [r[:, 0:4 * U].rearrange("p (m s) -> p m s", m=4) for r in (qkv0, qkv1)]
        K = [r[:, 4 * U:6 * U].rearrange("p (m s) -> p m s", m=2) for r in (qkv0, qkv1)]
        V = [r[:, 6 * U:8 * U].rearrange("p (t c) -> p t c", t=NT) for r in (qkv0, qkv1)]
        xnorm = {"in": yT_flat.rearrange("p (t d) -> p t d", t=NT),
                 "1": qkv0.rearrange("p (t d) -> p t d", t=NT),
                 "2": qkv0.rearrange("p (t d) -> p t d", t=NT),
                 "3": qkv0.rearrange("p (t d) -> p t d", t=NT)}
        big_w = qkv1.rearrange("p (k c) -> p k c", k=KD)
        probs = probs_flat.rearrange("p (n m s) -> p n m s", n=2, m=2)
        probsT = pT_flat.rearrange("p (n k q) -> p n k q", n=2, k=8)
        z = conv_flat[:, 0:2 * (S + PAD)].rearrange("p (c s) -> p c s", c=2)
        zc = conv_flat[:, 2 * (S + PAD):2 * (S + PAD) + 2 * S].rearrange("p (c s) -> p c s", c=2)
        res_tmp = pT_flat.rearrange("p (n d) -> p n d", n=2)
        tri_ones = misc[:, 0:640]

        ident = sb("ident", [P, P])
        ident_b = sb("ident_b", [P, P], BF16)
        mask_chunk = sb("mask_chunk", [P, P], BF16)
        mask_causal = sb("mask_causal", [P, P], BF16)
        mask_prev = sb("mask_prev", [P, P], BF16)
        rows = conv_flat[:, 0:P]
        sig = probs_flat.rearrange("p (c s) -> p c s", c=4)
        cols = sb("cols", [P, N_ROWS])
        lamv = probs_flat[:, 3 * U + P:3 * U + 2 * P].rearrange("p (n c) -> p n c", n=4)
        lam = sb("lam", [P, 8])
        sink = sb("sink", [P, 4])
        nsink = sb("nsink", [P, 4])
        foxb = sb("foxb", [P, 4])
        subg = sb("subg", [P, 1])
        blk_ones = probs_flat[:, 3 * U:3 * U + P]
        cln_x = probs_flat[:, 0:2 * U].rearrange("p (h n c) -> p h n c", h=2, n=4)
        squares = pT_flat.rearrange("p (c s) -> p c s", c=2)
        root = conv_flat[:, 0:2 * U].rearrange("p (c s) -> p c s", c=2)
        mem_nat = conv_flat[:, 0:2 * U].rearrange("p (n d) -> p n d", n=2)
        memT = probs_flat[:, 0:2 * U].rearrange("p (k m) -> p k m", k=KD)
        kmT = conv_flat[:, 0:2 * U].rearrange("p (k m) -> p k m", k=KD)
        vm = conv_flat[:, 2 * U:4 * U].rearrange("p (n d) -> p n d", n=2)
        qxT = qkv0.rearrange("p (k s) -> p k s", k=KD)
        xprobs = probs_flat[:, 2 * U:4 * U].rearrange("p (n t m) -> p n t m", n=2, t=4)
        xprobsT = pT_flat.rearrange("p (n m q) -> p n m q", n=2, m=2)
        stats = sb("stats", [P, NT, 2, 6])
        mv = sb("mv", [P, NT, 2])
        rstd = sb("rstd", [P, NT])
        negm = sb("negm", [P, 2, 2])
        sums = sb("sums", [P, 2, 2])
        rsum = sb("rsum", [P, 2, 4])
        xneg, xsum = sb("xneg", [P, 2, 4]), sb("xsum", [P, 2, 4])
        logf = sb("logf", [P, 2, NT, 4])
        fstat = gb[:, 0:NT * P].rearrange("p (t c) -> p t c", t=NT)
        cumT = gb[:, U:2 * U]

        psum = ctx.enter_context(nc.psum_tensor("psum", [P, 8, 512], F32))
        wide = [psum[:, 2 * n:2 * n + 2, :].rearrange("p a b -> p (a b)") for n in range(2)]
        ptb = [psum[:, 4 + n, :] for n in range(2)]
        obank = psum[:, 6, :]
        sbank = psum[:, 7, :]
        rms_psum = [psum[:, 6 - 2 * n:8 - 2 * n, :].rearrange("p a b -> p (a b)") for n in range(2)]

        x_loaded = [sem(f"x_loaded{t}") for t in range(NT)]
        rows_loaded = sem("rows_loaded")
        params_loaded = sem("params_loaded")
        gb_loaded = sem("gb_loaded")
        w_loaded = [sem(f"w_loaded{n}") for n in range(N_W)]
        consts_ready = sem("consts_ready")
        pool_step = sem("pool_step")
        q_zeroed = sem("q_zeroed")
        dve_step = sem("dve_step")
        act_step = sem("act_step")
        ln_stat = sem("ln_stat")
        ln_std = sem("ln_std")
        ln_done = sem("ln_done")
        res_ready = sem("res_ready")
        res_stored = [sem(f"res_stored{n}") for n in range(2)]
        wide_full = sem("wide_full")
        wide_read = sem("wide_read")
        pt_full = sem("pt_full")
        pt_copied = sem("pt_copied")
        row_max = sem("row_max")
        probs_ready = sem("probs_ready")
        pv_done = sem("pv_done")
        o_read = sem("o_read")
        glu_done = sem("glu_done")
        lam_sum = sem("lam_sum")
        lam_exp = sem("lam_exp")
        fox_z = sem("fox_z")
        fox_e = sem("fox_e")
        fox_l = sem("fox_l")
        fstat_ready = sem("fstat_ready")
        cum_full = sem("cum_full")
        aug_ready = sem("aug_ready")
        bigw_loaded = sem("bigw_loaded")

        w_in = ins["w_in"].rearrange("o (k p) n -> p (o k) n", p=P)
        xq = ins["xq"].rearrange("o (k p) n -> p (o k) n", p=P)
        xkv = ins["xkv"].rearrange("o (k p) n -> p (o k) n", p=P)

        def slot_view(n, width):
            return w_ring[:, n, 0:KD * width].rearrange("p (k c) -> p k c", k=KD)

        w_loads = []
        use_of = {}

        def add_load(width, parts, users):
            for u in users:
                use_of[u] = len(w_loads)
            w_loads.append((width, parts))

        def cols_of(src, c, n):
            return src[:, :, c:c + n]

        for c in range(2):
            add_load(256, [(0, 128, cols_of(w_in, C_CU + 128 * c, 128)),
                           (128, 128, cols_of(w_in, C_CU + 256 + 128 * c, 128))], [("a", c), ("g", c)])
        add_load(256, [(0, 128, cols_of(w_in, C_AQ, 128)), (128, 128, cols_of(w_in, C_AK, 128))],
                 [("q", 0), ("k", 0)])
        add_load(256, [(0, 256, cols_of(w_in, C_AV, 256))], [("v", 0, 0), ("v", 0, 1)])
        add_load(256, [(0, 128, cols_of(w_in, C_AQ + 128, 128)), (128, 128, cols_of(w_in, C_AK + 128, 128))],
                 [("q", 1), ("k", 1)])
        add_load(256, [(0, 64, cols_of(w_in, C_SQ, 64)), (64, 64, cols_of(w_in, C_SQ + 128, 64)),
                       (128, 64, cols_of(w_in, C_SQ + 64, 64)), (192, 64, cols_of(w_in, C_SQ + 192, 64))],
                 [("q", 2), ("q", 3)])
        add_load(256, [(0, 256, cols_of(w_in, C_SK, 256))], [("k", 2), ("v", 2, 0)])
        add_load(256, [(0, 128, cols_of(w_in, C_FQ, 128)), (128, 128, cols_of(w_in, C_FK, 128))],
                 [("q", 4), ("k", 4)])
        add_load(260, [(0, 260, cols_of(w_in, C_FV, 260))], [("v", 4, n) for n in range(4)])
        add_load(256, [(0, 128, cols_of(w_in, C_FQ + 128, 128)), (128, 128, cols_of(w_in, C_FK + 128, 128))],
                 [("q", 5), ("k", 5)])
        for n in range(8):
            add_load(256, [(0, 256, cols_of(xkv, 256 * n, 256))], [("m", n)])
        for n in range(4):
            add_load(256, [(0, 256, cols_of(xq, 256 * n, 256))], [("xq", 2 * n), ("xq", 2 * n + 1)])
        add_load(256, [(0, 256, ins["sh_wg"].rearrange("o (k p) n -> p (o k) n", p=P))], [("sg", 0), ("sg", 1)])
        add_load(256, [(0, 256, ins["sh_wu"].rearrange("o (k p) n -> p (o k) n", p=P))], [("su", 0), ("su", 1)])
        add_load(256, [(0, 256, None)], [("sd", 0)])

        all_items = dict(item_of)
        for n in range(8):
            all_items[("m", n)] = IT_MEM + n // 2
            all_items[("xq", n)] = IT_XQ + n
        for m in range(2):
            all_items[("sg", m)] = IT_SH + 2 * m
            all_items[("su", m)] = IT_SH + 2 * m + 1
        last_item = [max(all_items[u] for u in use_of if use_of[u] == n) for n in range(len(w_loads) - 1)]
        RMS_OF = {}
        n_max = 0
        for s in range(NS):
            for m in range(2 if STEPS[s][1] == "diff" else 1):
                RMS_OF[(s, m)] = n_max
                n_max += 1
        SLOT_OF = {0: 0, 1: 1, 2: 0, 3: 1, 4: 0}
        Q_ZEROED = {0: 1, 1: 2, 2: 3, 3: 4, 4: 5}
        Y_CHUNK = {"diff": 0, "swa": 4, "fox": 6}
        VAL = {"diff": V[0], "swa": V[1], "fox": V[0]}

        w_count, per_slot = [], [0] * N_W
        for n, (_, parts) in enumerate(w_loads):
            per_slot[n % N_W] += 16 * len(parts)
            w_count.append(per_slot[n % N_W])

        conv_done = sem("conv_done")
        cln_full, cln_stat, cln_std, cln_xn = sem("cln_full"), sem("cln_stat"), sem("cln_std"), sem("cln_xn")
        cln_back, cln_act = sem("cln_back"), sem("cln_act")
        sq_ready, rms_full, rms_root, rms_done = sem("sq_ready"), sem("rms_full"), sem("rms_root"), sem("rms_done")
        rms_log, blk_ready = sem("rms_log"), sem("blk_ready")
        mem_loaded = sem("mem_loaded")
        mix_full, mix_read = sem("mix_full"), sem("mix_read")
        xmax, xprobs_ready = sem("xmax"), sem("xprobs_ready")
        rw_loaded, routed = sem("rw_loaded"), sem("routed")
        rank_full, blk_full = sem("rank_full"), sem("blk_full")
        table_ready = sem("table_ready")
        hs_ready = sem("hs_ready")
        acc_stored = sem("acc_stored")
        h_stored = sem("h_stored")
        out_stored = sem("out_stored")
        gu_loaded = [sem(f"gu_loaded{n}") for n in range(2)]
        wd_loaded = [sem(f"wd_loaded{n}") for n in range(2)]
        onehot_ready, idx_full, idx_ready = sem("onehot_ready"), sem("idx_full"), sem("idx_ready")
        gathered = [sem(f"gathered{n}") for n in range(2)]
        xt_full, xt_rounded, xt_copied = sem("xt_full"), sem("xt_rounded"), sem("xt_copied")
        h_split, xw_rounded, xw_split = sem("h_split"), sem("xw_rounded"), sem("xw_split")
        o_rounded, o_split, xo_rounded, xo_split = (sem("o_rounded"), sem("o_split"), sem("xo_rounded"),
                                                    sem("xo_split"))
        gu_rounded, gu_split = sem("gu_rounded"), sem("gu_split")
        gu_full, silu_done, h_ready = sem("gu_full"), sem("silu_done"), sem("h_ready")
        ht_full, ht_copied = sem("ht_full"), sem("ht_copied")
        y_full, y_ready, scattered = sem("y_full"), sem("y_ready"), sem("scattered")
        moe_setup, moe_step = sem("moe_setup"), sem("moe_step")
        pool_pace, sp_pace, out_scale = sem("pool_pace"), sem("sp_pace"), sem("out_scale")
        out_norm = sem("out_norm")

        rw = misc[:, 0:KD * N_EXP].rearrange("p (k e) -> p k e", k=KD)
        rbias = misc[:, KD * N_EXP:KD * N_EXP + N_EXP]
        logitsT = probs_flat[0:N_EXP, 0:U]
        hs = yT_flat[:, 6 * U:8 * U].rearrange("p (k s) -> p k s", k=2)
        hs_tmp = probs_flat[:, U:2 * U]
        r_all = conv_flat
        rs_scores = r_all[:, 0:512].rearrange("p (t e) -> p t e", t=NT)
        rs_choice = r_all[:, 512:512 + NT * 66].rearrange("p (t e) -> p t e", t=NT)
        rs_sel = r_all[:, 1040:1552].rearrange("p (t e) -> p t e", t=NT)
        rs_gate = r_all[:, 1552:2064].rearrange("p (t e) -> p t e", t=NT)
        rs_rank = r_all[:, 2576:3088].rearrange("p (t e) -> p t e", t=NT)
        rs_off = r_all[:, 3088:3088 + 576].rearrange("p (t e) -> p t e", t=NT + 1)
        rs_selb = r_all[:, 3664:3920].bitcast(BF16).rearrange("p (t e) -> p t e", t=NT)
        small = pT_flat[:, U:2 * U]
        top8 = small[:, 0:512].rearrange("p (t g n) -> p t g n", t=NT, g=N_GRP)
        gsum = small[:, 512:608].rearrange("p (t g) -> p t g", t=NT)
        gtop = small[:, 608:672].rearrange("p (t g) -> p t g", t=NT)
        gpen = small[:, 672:736].rearrange("p (t g) -> p t g", t=NT)
        gden = small[:, 736:752].rearrange("p (t g) -> p t g", t=NT)
        nb_i = small[:, 752:816].bitcast(I32)
        turn_i = small[:, 1008:1009].bitcast(I32)
        blk_row = small[0:1, 0:2 * P]
        nb_f = small[:, 816:1008].rearrange("p (n e) -> p n e", n=3)
        tri_b = sb("tri_b", [P, P], BF16)
        ones_b = sb("ones_b", [P, P], BF16)
        iota_s = sb("iota_s", [P, P])
        pcol = sb("pcol", [P, 4])
        blk_exp = sb("blk_exp", [P, 2])
        STREAM1, TURNS, FRESH = P, 2 * P, 2 * P + 8
        table = misc[0:1, 0:FRESH + 2 * P].bitcast(I32)
        dest = qkv1[:, 6 * U:6 * U + 512].rearrange("p (e t) -> p e t", e=N_EXP)
        gparts = qkv1[:, 7 * U:7 * U + 768].bitcast(BF16).rearrange("p (e t g) -> p e t g", e=N_EXP, t=NT)
        onehot = conv_flat[:, 0:U].bitcast(BF16).rearrange("p (n t r) -> p n t r", n=2, t=NT)
        h_exp = conv_flat[:, U:U + 512].rearrange("p (n f) -> p n f", n=2)
        hT_exp = conv_flat[:, U + 512:2 * U].rearrange("p (n k r) -> p n k r", n=2, k=2)
        xg = probs_flat[:, 0:2 * U].rearrange("p (n d) -> p n d", n=2)
        y_exp = pT_flat.rearrange("p (n d) -> p n d", n=2)
        slot_cols = sb("slot_cols", [P, 2, NT, 6], BF16)
        d8 = sb("d8", [P, NT])
        blk_base = sb("blk_base", [P, 2])
        idx_new = sb("idx_new", [P, 2], I32)
        gate_new = sb("gate_new", [P, 2])
        idx_now = sb("idx_now", [P, 2], I32)
        gate_now = sb("gate_now", [P, 2])
        idx_tmp = sb("idx_tmp", [P, 2, 2])
        nbias = xneg.rearrange("p n t -> p (n t)")
        exp_w = [r[:, 0:6 * U] for r in (qkv1, yT_flat)]
        wd_w = [r[:, 4 * U:6 * U].rearrange("p (k c) -> p k c", k=2) for r in exp_w]
        h_raw = placed("h_raw", 8 * U, KD, S, dt=F32)
        h_hi, h_lo = placed("h_hi", 0, KD, S), placed("h_lo", 8 * U, KD, S)
        xw_raw = placed("xw_raw", 42 * U + 64 + 640, N_W, W_SLOT, dt=F32)
        xw_hi, xw_lo = placed("xw_hi", 24 * U, 2, KD, 256), placed("xw_lo", 28 * U, 2, KD, 256)
        XQ_LOAD = use_of[("xq", 0)]
        XO_SPLIT = KD - 2
        o_raw, xo_raw = placed("o_raw", 8 * U, KD, S, dt=F32), placed("xo_raw", 24 * U, KD, D, dt=F32)
        o_hi, o_lo = placed("o_hi", 42 * U + 64 + 640, XO_SPLIT, S), placed("o_lo", 8 * U, XO_SPLIT, S)
        xo_hi, xo_lo = placed("xo_hi", 0, XO_SPLIT, D), placed("xo_lo", 24 * U, XO_SPLIT, D)
        GU_AT = (24 * U, 8 * U)
        gu_w = [placed(f"gu_w{n}", GU_AT[n], KD, 2 * D_EXP, dt=F32) for n in range(2)]
        gu_hi = [placed(f"gu_hi{n}", 4 * U * n, KD, 2 * D_EXP) for n in range(2)]
        gu_lo = [placed(f"gu_lo{n}", 16 * U + 4 * U * n, KD, 2 * D_EXP) for n in range(2)]
        xgT_hi = placed("xgT_hi", 34 * U, 2, KD, P)
        xgT_lo = placed("xgT_lo", 14 * U, 2, KD, P)
        GU_PARTS = 4
        A_SPLIT, V_SPLIT = 4, 3
        MAX_TURNS = (MAX_BLOCKS + 1) // 2

        block = ctx.enter_context(nc.Block())

        def bcast(name, n):
            return ins[name].rearrange("(o n) -> o n", o=1).broadcast_to([P, n]) \
                if len(ins[name].shape) == 1 else ins[name].broadcast_to([P, n])

        @block.sync
        def _(sp):
            x_dram = ins["x"].rearrange("b (t p) d -> t p (b d)", p=P)
            res_dram = h_res.rearrange("(t p) d -> t p d", p=P)
            table_dram = h_table.rearrange("(t p) d -> t p d", p=P)
            acc_dram = acc.rearrange("(t p) d -> t p d", p=P)
            out_dram = out.rearrange("b (t p) d -> t p (b d)", p=P)
            for t in range(4):
                sp.dma_start(xnorm["in"][:, t, :], x_dram[t]).then_inc(x_loaded[t], 16)
            def param_rows(row, src):
                sp.dma_start(rows[row:row + src.shape[0], 0:src.shape[1]], src).then_inc(rows_loaded, 16)

            for r, g, b in ((0, "ln_in_g", "ln_in_b"), (16, "ln1_g", "ln1_b"), (32, "ln2_g", "ln2_b")):
                for row, name in ((r, g), (r + 8, b)):
                    src = ins[name]
                    src = src.rearrange("(k p) -> k p", p=P) if len(src.shape) == 1 \
                        else src.rearrange("o (k p) -> (o k) p", p=P)
                    param_rows(row, src)
            for row, name in ((R_CONVB, "conv_b"), (R_CLNG, "conv_ln_g"), (R_CLNB, "conv_ln_b")):
                param_rows(row, ins[name].rearrange("o (k p) -> (o k) p", p=P))
            for half in range(2):
                sp.dma_start(rows[R_SUBG:R_SUBG + 1, 64 * half:64 * half + 64],
                             ins["diff_subln_g"]).then_inc(rows_loaded, 16)
            for c in range(2):
                param_rows(R_CONVW + CONV_K * c, ins["conv_w"][0, :, P * c:P * c + P])
            for t in range(4, NT):
                sp.dma_start(xnorm["in"][:, t, :], x_dram[t]).then_inc(x_loaded[t], 16)
            for n, name in enumerate(("diff_lq1", "diff_lk1", "diff_lq2", "diff_lk2")):
                sp.dma_start(lamv[:, n, :], bcast(name, 32)).then_inc(params_loaded, 16)
            sp.dma_start(sink[:, :], bcast("swa_sink", 4)).then_inc(params_loaded, 16)
            sp.dma_start(foxb[:, :], bcast("fox_fb", 4)).then_inc(params_loaded, 16)

            def load_gb(g, b):
                sp.dma_start(gb[:, 0:U], bcast(g, D)).then_inc(gb_loaded, 16)
                sp.dma_start(gb[:, U:2 * U], bcast(b, D)).then_inc(gb_loaded, 16)

            load_gb("ln_in_g", "ln_in_b")

            def store_residual(ln):
                for t in range(NT):
                    sp.wait_ge(res_ready, NT * ln + t + 1)
                    sp.dma_start(res_dram[t], res_tmp[:, t % 2, :]).then_inc(res_stored[t % 2], 16)

            def load_residual(ln):
                for n in range(2):
                    sp.wait_ge(res_stored[n], 16 * ln * NT // 2)
                for t in range(NT):
                    sp.dma_start(xnorm[str(ln)][:, t, :], res_dram[t]).then_inc(x_loaded[t], 16)

            def load_w(n):
                width, parts = w_loads[n]
                if n >= N_W:
                    sp.wait_ge(wide_full, last_item[n - N_W] + 1)
                if n == len(w_loads) - 1:
                    sp.dma_start(w_ring[:, n % N_W, 0:2 * D].rearrange("p (k c) -> p k c", k=2),
                                 ins["sh_wd"].rearrange("o (k p) c -> p (o k) c", p=P)
                                 ).then_inc(w_loaded[n % N_W], 16)
                    return
                slot = slot_view(n % N_W, width)
                if XQ_LOAD <= n < XQ_LOAD + 4:
                    slot = xw_raw[:, n % N_W, 0:KD * width].rearrange("p (k c) -> p k c", k=KD)
                for c, m, src in parts:
                    sp.dma_start(slot[:, :, c:c + m], src).then_inc(w_loaded[n % N_W], 16)

            for n in range(N_W):
                load_w(n)
            store_residual(0)
            for n in range(N_W, 10):
                load_w(n)
            first4 = STEPS.index((4, "fox", 1, 0, 0))
            sp.wait_ge(pv_done, first4)
            sp.dma_start(big_w, ins["w_out"].rearrange("o (k p) c -> p (o k) c", p=P)).then_inc(bigw_loaded, 16)
            sp.wait_ge(aug_ready, 2)
            load_gb("ln1_g", "ln1_b")
            sp.wait_ge(pv_done, NS)
            load_residual(1)
            for n in range(10, 12):
                load_w(n)
            sp.wait_ge(rms_done, 2)
            for n in range(2):
                sp.dma_start(mem_nat[:, n, :], ins["mem"][0, P * n:P * n + P, :]).then_inc(mem_loaded, 16)
            load_w(12)
            store_residual(1)
            for n in range(13, 22):
                load_w(n)
            sp.wait_ge(wide_full, IT_XQ + 8)
            sp.dma_start(xo_raw[:, :, :], ins["xo"].rearrange("o (k p) c -> p (o k) c", p=P)).then_inc(bigw_loaded, 16)
            load_gb("ln2_g", "ln2_b")
            sp.dma_start(rw[:, :, :], ins["router_w"].rearrange("o (k p) e -> p (o k) e", p=P)).then_inc(rw_loaded, 16)
            sp.dma_start(rbias, bcast("router_bias", N_EXP)).then_inc(rw_loaded, 16)
            sp.wait_ge(wide_full, x_item[("xs", 7)] + 1)
            load_residual(2)
            sp.wait_ge(mix_full, 2 * NT)
            for n in range(22, 25):
                load_w(n)
            for t in range(NT):
                sp.wait_ge(res_ready, NT * 2 + t + 1)
                sp.dma_start(table_dram[t], xnorm["2"][:, t, :]).then_inc(h_stored, 16)
            exp_gu = [ins[n].rearrange("o e (k p) f -> (o e) p k f", p=P) for n in ("exp_wg", "exp_wu")]
            exp_d = ins["exp_wd"].rearrange("o e (k p) c -> (o e) p k c", p=P)

            def load_expert(e, slot):
                for n in range(2):
                    sp.dma_start(gu_w[slot][:, :, D_EXP * n:D_EXP * n + D_EXP],
                                 exp_gu[n][bass.ds(e, 1)].rearrange("o p k f -> p (o k) f")
                                 ).then_inc(gu_loaded[slot], 16)

            def load_expert_down(e, slot):
                sp.dma_start(wd_w[slot], exp_d[bass.ds(e, 1)].rearrange("o p k c -> p (o k) c")
                             ).then_inc(wd_loaded[slot], 16)

            sp.wait_ge(table_ready, 1)
            for b in range(2):
                e = sp.value_load(table[0:1, STREAM1 * b:STREAM1 * b + 1], min_val=0, max_val=N_EXP - 1)
                load_expert(e, b)
                if b == 0:
                    sp.wait_ge(idx_ready, 2)
                load_expert_down(e, b)
            turns = sp.value_load(table[0:1, TURNS:TURNS + 1], min_val=1, max_val=MAX_TURNS)
            with sp.Fori(0, turns) as i:
                for b in range(2):
                    e = sp.value_load(table[0:1, bass.ds(i + 1 + STREAM1 * b, 1)], min_val=0, max_val=N_EXP - 1)
                    fresh = sp.value_load(table[0:1, bass.ds(i + FRESH + STREAM1 * b, 1)], min_val=0, max_val=1)
                    sp.wait_ge(gu_split, 2 * GU_PARTS * i + GU_PARTS * (b + 1))
                    sp.sem_inc(sp_pace, 1)
                    with sp.If(fresh == 1):
                        load_expert(e, b)
                    with sp.If(fresh == 0):
                        sp.sem_inc(gu_loaded[b], 32)
                    sp.wait_ge(y_full, 2 * i + b + 1)
                    sp.sem_inc(sp_pace, 1)
                    with sp.If(fresh == 1):
                        load_expert_down(e, b)
                    with sp.If(fresh == 0):
                        sp.sem_inc(wd_loaded[b], 16)
            for b in range(2):
                sp.wait_ge(gu_loaded[b], 32 * turns + 32)
                sp.wait_ge(wd_loaded[b], 16 * turns + 16)
            load_gb("ln3_g", "ln3_b")
            sp.wait_ge(scattered, 32 * turns + 32)
            sp.wait_ge(gu_split, 2 * GU_PARTS * turns + GU_PARTS)
            for t in range(NT):
                sp.dma_start(xnorm["3"][:, t, :], acc_dram[t]).then_inc(x_loaded[t], 16)
            for t in range(NT):
                sp.wait_ge(res_ready, NT * 3 + t + 1)
                sp.dma_start(out_dram[t], xnorm["3"][:, t, :]).then_inc(out_stored, 16)
            sp.wait_ge(out_stored, 16 * NT)

        @block.gpsimd
        def _(pool):
            chain = [0]

            def link(made):
                chain[0] += 1
                made.then_inc(pool_step, 1)
                pool.wait_ge(pool_step, chain[0])

            def select(t, fill, pattern, mult, op, base=0):
                return nc.gpsimd.affine_select(out=t, in_=t, pattern=pattern, compare_op=op,
                                               fill=fill, base=base, channel_multiplier=mult)

            link(nc.gpsimd.memset(ident[:, :], 0.0))
            link(select(ident[:, :], 1.0, [[-1, P]], 1, ALU.not_equal))
            nc.gpsimd.tensor_copy(ident_b[:, :], ident[:, :]).then_inc(consts_ready, 1)
            link(nc.gpsimd.memset(mask_causal[:, :], 0.0))
            select(mask_causal[:, :], NEG, [[-1, P]], 1, ALU.is_ge).then_inc(consts_ready, 1)
            link(nc.gpsimd.memset(mask_chunk[:, :], 0.0))
            nc.gpsimd.memset(mask_chunk[0:CHUNK, CHUNK:P], NEG).then_inc(consts_ready, 1)
            link(nc.gpsimd.memset(mask_prev[:, :], NEG))
            nc.gpsimd.memset(mask_prev[0:CHUNK, CHUNK:P], 0.0).then_inc(consts_ready, 1)
            nc.gpsimd.memset(qkv0[:, 0:4 * U], 0.0).then_inc(q_zeroed, 1)
            nc.gpsimd.memset(qkv1[:, 0:4 * U], 0.0).then_inc(q_zeroed, 1)
            def residual(ln, staged):
                pool.wait_ge(gb_loaded, 32 * (ln + 1))
                if staged:
                    link(nc.gpsimd.tensor_scalar(gb[:, :], gb[:, :], ALPHA, None, ALU.mult))
                src = xnorm["in"] if ln == 0 else xnorm[str(ln)]
                for t in range(NT):
                    pool.wait_ge(ln_done, NT * ln + t + 1)
                    if staged:
                        if NT * ln + t >= 2:
                            pool.wait_ge(res_stored[t % 2], 16 * ((NT * ln + t) // 2))
                        dst = res_tmp[:, t % 2, :]
                    else:
                        dst = src[:, t, :]
                    link(nc.gpsimd.tensor_tensor(dst, src[:, t, :], gb[:, 0:U], ALU.mult))
                    nc.gpsimd.tensor_tensor(dst, dst, gb[:, U:2 * U], ALU.add).then_inc(res_ready, 1)

            residual(0, True)
            link(nc.gpsimd.memset(tri_ones, 1.0))
            select(tri_ones[:, 0:P], 0.0, [[1, P]], -1, ALU.is_ge).then_inc(consts_ready, 1)
            for group, q in ((2, 4), (3, 4), (4, 2)):
                prev = [s for s in range(NS) if STEPS[s][0] == group - 2]
                pool.wait_ge(wide_full, item_of[("s", prev[-1], 1 if group - 2 < 2 else 0)] + 1)
                region = (qkv0, qkv1)[SLOT_OF[group]]
                zero = nc.gpsimd.memset(region[:, 0:q * U], 0.0)
                if group == 2:
                    zero.then_inc(q_zeroed, 1)
                else:
                    link(zero)
                    link(nc.gpsimd.memset(region[:, 4 * U:6 * U], 0.0))
                    for p in range(2):
                        row = (64, 0)[p]
                        link(nc.gpsimd.memset(Q[SLOT_OF[group]][row + 32:row + 33, p, :], 1.0))
                        link(nc.gpsimd.memset(K[SLOT_OF[group]][row:row + 1, p, :], 1.0))
                    pool.sem_inc(q_zeroed, 1)
            link(nc.gpsimd.memset(tri_b[:, :], 1.0))
            select(tri_b[:, :], 0.0, [[1, P]], -1, ALU.is_gt).then_inc(consts_ready, 1)
            nc.gpsimd.memset(ones_b[:, :], 1.0).then_inc(consts_ready, 1)
            nc.gpsimd.iota(iota_s[:, :], [[1, P]], base=0, channel_multiplier=0,
                           allow_small_or_imprecise_dtypes=True).then_inc(consts_ready, 1)
            for n, (base, mult) in enumerate(((0, 1), (-S, -1), (S, 1))):
                nc.gpsimd.iota(pcol[:, n:n + 1], [[0, 1]], base=base, channel_multiplier=mult,
                               allow_small_or_imprecise_dtypes=True).then_inc(consts_ready, 1)
            for b in range(2):
                nc.gpsimd.iota(slot_cols[:, b, :, 0], [[P, NT]], base=0, channel_multiplier=0,
                               allow_small_or_imprecise_dtypes=True).then_inc(consts_ready, 1)
                nc.gpsimd.iota(slot_cols[:, b, :, 1], [[0, NT]], base=0, channel_multiplier=1,
                               allow_small_or_imprecise_dtypes=True).then_inc(consts_ready, 1)
                nc.gpsimd.memset(slot_cols[:, b, :, 2], 1.0).then_inc(consts_ready, 1)
            pool.wait_ge(rms_full, 2)
            residual(1, True)
            pool.wait_ge(pt_full, CH_LN["2", 1] + KD)
            residual(2, False)

            pool.wait_ge(moe_setup, 1)
            pool.dma_start(h_table[S:S + P, :], y_exp[:, 0, :]).then_inc(scattered, 16)
            pool.wait_ge(scattered, 16)
            pool.dma_start(acc[S:S + P, :], y_exp[:, 0, :]).then_inc(scattered, 16)
            pool.wait_ge(scattered, 32)
            pool.wait_ge(h_stored, 16 * NT)

            def gather(slot):
                pool.indirect_dma_start(xg[:, slot, :], None, h_table[:, :],
                                        bass.IndirectOffsetOnAxis(ap=idx_new[:, slot:slot + 1], axis=0)
                                        ).then_inc(gathered[slot], 16)

            for j in range(2):
                pool.wait_ge(idx_ready, j + 1)
                gather(j)
            pool.wait_ge(acc_stored, 16 * NT)
            turns = pool.value_load(table[0:1, TURNS:TURNS + 1], min_val=1, max_val=MAX_TURNS)
            with pool.Fori(0, turns) as i:
                for b in range(2):
                    pool.wait_ge(idx_ready, 2 * i + b + 3)
                    pool.sem_inc(pool_pace, 1)
                    pool.wait_ge(xt_full, 4 * i + 2 * b + 2)
                    pool.sem_inc(pool_pace, 1)
                    gather(b)
                    pool.wait_ge(scattered, 32 * i + 16 * b + 32)
                    pool.sem_inc(pool_pace, 1)
                    pool.wait_ge(y_ready, 2 * i + b + 2)
                    pool.sem_inc(pool_pace, 1)
                    pool.indirect_dma_start(acc[:, :], bass.IndirectOffsetOnAxis(ap=idx_now[:, b:b + 1], axis=0),
                                            y_exp[:, b, :], None, compute_op=ALU.add).then_inc(scattered, 16)
            pool.wait_ge(scattered, 32 * turns + 32)
            pool.sem_inc(pool_pace, 1)
            for b in range(2):
                pool.wait_ge(gathered[b], 16 * turns + 16)
                pool.sem_inc(pool_pace, 1)
            pool.wait_ge(gb_loaded, 128)
            for t in range(NT):
                pool.wait_ge(ln_done, NT * 3 + t + 1)
                nc.gpsimd.tensor_tensor(xnorm["3"][:, t, :], xnorm["3"][:, t, :], gb[:, U:2 * U],
                                        ALU.add).then_inc(res_ready, 1)

        @block.tensor
        def _(pe):
            def transposes(chunk, blocks):
                if chunk >= 2:
                    pe.wait_ge(pt_copied, chunk - 1)
                for dst, src in blocks:
                    mm = nc.tensor.transpose(dst, src, ident[0:src.shape[0], 0:src.shape[0]])
                mm.then_inc(pt_full, 1)

            pe.wait_ge(rows_loaded, 16 * 13)
            pe.wait_ge(pool_step, 2)
            pe.wait_ge(consts_ready, 4)
            transposes(0, [(ptb[0][:, 0:N_ROWS], rows[0:N_ROWS, :])])

            def ln_transposes(which, half, done):
                pe.wait_ge(ln_done, done)
                for k in range(KD):
                    c = CH_LN[which, half] + k
                    transposes(c, [(ptb[c % 2][:, P * n:P * n + P],
                                    xnorm[which][:, 4 * half + n, P * k:P * k + P]) for n in range(4)])

            ln_transposes("in", 0, 4)

            def weights(what):
                load = use_of[what]
                pe.wait_ge(w_loaded[load % N_W], w_count[load])
                return slot_view(load % N_W, w_loads[load][0])

            def transposed_projection(dst, w, c0, m=P, halves=(0, 1)):
                for half in halves:
                    for k in range(KD):
                        mm = nc.tensor.matmul(dst[0:m, HALF * half:HALF * half + HALF], w[:, k, c0:c0 + m],
                                              hT[:, k, HALF * half:HALF * half + HALF],
                                              start=(k == 0), stop=(k == KD - 1))
                return mm

            def projection(what):
                item = item_of[what]
                w = weights(what)
                if what == ("a", 0):
                    pe.wait_ge(pt_copied, 1 + KD)
                    transposed_projection(wide[item % 2], w, 0, halves=(0,))
                    ln_transposes("in", 1, 8)
                    pe.wait_ge(pt_copied, 1 + LN_CHUNKS)
                    transposed_projection(wide[item % 2], w, 0, halves=(1,)).then_inc(wide_full, 1)
                    return
                if item >= 2:
                    pe.wait_ge(wide_read, item - 1)
                dst = wide[item % 2]
                if what[0] == "v":
                    if what[1] == 0:
                        tiles, n0, n, stride = range(4 * what[2], 4 * what[2] + 4), 0, 256, 256
                    elif what[1] == 2:
                        tiles, n0, n, stride = range(NT), 128, 128, 128
                    else:
                        tiles, n0, n, stride = range(2 * what[2], 2 * what[2] + 2), 0, 260, 512
                    for a, t in enumerate(tiles):
                        for k in range(KD):
                            mm = nc.tensor.matmul(dst[:, a * stride:a * stride + n], hT[:, k, P * t:P * t + P],
                                                  w[:, k, n0:n0 + n], start=(k == 0), stop=(k == KD - 1))
                else:
                    second = what[0] == "g" or (what[0] == "k" and what[1] != 2) or what == ("q", 3)
                    mm = transposed_projection(dst, w, P if second else 0)
                mm.then_inc(wide_full, 1)

            def scores(s):
                group, kind, pair, parity, tile = STEPS[s]
                keys = key_tiles(kind, tile)
                slot = SLOT_OF[group]
                pe.wait_ge(wide_read, GROUP_READY[group] + 1)
                if kind == "fox":
                    pe.wait_ge(aug_ready, group - 2)
                for m in range(2 if kind == "diff" else 1):
                    item = item_of[("s", s, m)]
                    pe.wait_ge(wide_read, item - 1)
                    dst = wide[item % 2]
                    if kind == "diff":
                        q, k = Q[slot][:, 2 * parity + m, :], K[slot][:, 0, :]
                    elif kind == "swa":
                        q, k = Q[slot][:, 2 * pair + parity, :], K[slot][:, 0, :]
                    else:
                        q, k = Q[slot][:, parity, :], K[slot][:, parity, :]
                    n = P * len(keys)
                    for c in range(0, n, 512):
                        w = min(512, n - c)
                        nc.tensor.matmul(dst[:, c:c + w], q[:, P * tile:P * tile + P],
                                         k[:, P * keys[0] + c:P * keys[0] + c + w], start=True, stop=c + w < n)
                    if kind == "swa" and tile:
                        nc.tensor.matmul(dst[:, 0:P], ident_b[:, :], mask_prev[:, :], start=False, stop=False)
                    mm = nc.tensor.matmul(dst[:, n - P:n], ident_b[:, :],
                                          (mask_causal if kind == "fox" else mask_chunk)[:, :],
                                          start=False, stop=True)
                    mm.then_inc(wide_full, 1)

            def turn(s):
                _, kind, _, _, tile = STEPS[s]
                keys = key_tiles(kind, tile)
                pe.wait_ge(probs_ready, s + 1)
                parts = [keys[c:c + 4] for c in range(0, len(keys), 4)]
                for n, part in enumerate(parts):
                    c = chunk_of[s] + n
                    transposes(c, [(ptb[c % 2][:, P * b:P * b + P],
                                    probs[:, s % 2, 0, P * (4 * n + b):P * (4 * n + b) + P])
                                   for b in range(len(part))])

            def values(s):
                _, kind, pair, parity, tile = STEPS[s]
                keys = key_tiles(kind, tile)
                parts = [keys[c:c + 4] for c in range(0, len(keys), 4)]
                if s // 2 >= 2:
                    pe.wait_ge(o_read, s // 2 - 1)
                dst = (obank, sbank)[s // 2 % 2][64 * parity:64 * parity + 64, 0:P]
                vc = 64 * pair if kind == "swa" else P * pair + 64 * parity
                for n, part in enumerate(parts):
                    pe.wait_ge(pt_copied, chunk_of[s] + n + 1)
                    for b, kt in enumerate(part):
                        j = 4 * n + b
                        mm = nc.tensor.matmul(dst, VAL[kind][:, kt, vc:vc + 64], probsT[:, s % 2, j, :],
                                              start=(j == 0), stop=(j == len(keys) - 1))
                mm.then_inc(pv_done, 1)

            def cumulate():
                item = item_of["cum"]
                pe.wait_ge(fstat_ready, 1)
                pe.wait_ge(consts_ready, 5)
                pe.wait_ge(wide_read, item - 1)
                for half in range(2):
                    last = 4 * half + 3
                    for t in range(last + 1):
                        c0 = max(P * t, HALF * half)
                        n = HALF * (half + 1) - c0
                        src = tri_ones[:, 0:n] if P * t >= HALF * half else tri_ones[:, P:P + n]
                        mm = nc.tensor.matmul(wide[item % 2][:, c0:c0 + n], fstat[:, t, :], src,
                                              start=(t == 0), stop=(t == last))
                mm.then_inc(wide_full, 1)

            for kind, what in PLAN:
                if kind == "proj":
                    projection(what)
                elif kind == "cum":
                    cumulate()
                elif kind == "scores":
                    scores(what)
                elif kind == "turn":
                    turn(what)
                else:
                    values(what)

            pe.wait_ge(wide_read, ATT_ITEMS)
            pe.wait_ge(conv_done, 2 * CONV_K)
            for h in range(2):
                for n in range(4):
                    for c in range(2):
                        mm = nc.tensor.transpose(wide[h][:, 256 * n + P * c:256 * n + P * c + P],
                                                 zc[:, c, P * (4 * h + n):P * (4 * h + n) + P], ident[:, :])
                mm.then_inc(cln_full, 1)
            pe.wait_ge(blk_ready, 1)
            pe.wait_ge(pt_copied, ATT_CHUNKS)
            pe.wait_ge(o_read, NS // 2)
            for c in range(2):
                pe.wait_ge(sq_ready, c + 1)
                for half in range(2):
                    mm = nc.tensor.matmul(rms_psum[c][:, HALF * half:HALF * half + HALF], blk_ones,
                                          squares[:, c, HALF * half:HALF * half + HALF], start=True, stop=True)
                mm.then_inc(rms_full, 1)
            for h in range(2):
                pe.wait_ge(cln_xn, h + 1)
                for c in range(2):
                    for n in range(4):
                        mm = nc.tensor.transpose(wide[h][:, HALF * c + P * n:HALF * c + P * n + P],
                                                 cln_x[:, h, n, P * c:P * c + P], ident[:, :])
                mm.then_inc(cln_back, 1)

            def output_projection(tile):
                if tile >= 2:
                    pe.wait_ge(mix_read, tile - 1)
                for c in range(2):
                    for k in range(KD):
                        mm = nc.tensor.matmul(wide[tile % 2][:, HALF * c:HALF * c + HALF],
                                              yT[:, k, P * tile:P * tile + P],
                                              big_w[:, k, HALF * c:HALF * c + HALF],
                                              start=(k == 0), stop=(k == KD - 1))
                mm.then_inc(mix_full, 1)

            pe.wait_ge(bigw_loaded, 16)
            pe.wait_ge(cln_act, 2)
            pe.wait_ge(rms_done, 2)
            for t in range(5):
                output_projection(t)
            ln_transposes("1", 0, NT + 4)
            for t in range(5, NT):
                output_projection(t)
            pe.wait_ge(mem_loaded, 32)
            for n in range(4):
                c = CH_MEM + n
                transposes(c, [(ptb[c % 2][:, 256 * a + P * m:256 * a + P * m + P],
                                mem_nat[:, m, P * (2 * n + a):P * (2 * n + a) + P])
                               for a in range(2) for m in range(2)])
            pe.wait_ge(pt_copied, CH_MEM + 4)
            pe.wait_ge(mix_read, NT)
            for n in range(8):
                if n == 2:
                    ln_transposes("1", 1, NT + 8)
                w = weights(("m", n))
                item = IT_MEM + n // 2
                if n % 2 == 0:
                    pe.wait_ge(wide_read, item - 1)
                for a in range(2):
                    dst = wide[item % 2][:, HALF * (n % 2) + 256 * a:HALF * (n % 2) + 256 * a + 256]
                    for k in range(KD):
                        lhs, rhs = (w[:, k, P * a:P * a + P], memT[:, k, :]) if n < 4 \
                            else (memT[:, k, P * a:P * a + P], w[:, k, :])
                        mm = nc.tensor.matmul(dst, lhs, rhs, start=(k == 0), stop=(k == KD - 1))
                if n % 2:
                    mm.then_inc(wide_full, 1)
            pe.wait_ge(h_split, 2 * KD)
            for n in range(8):
                slot, c0 = n // 2 % 2, P * (n % 2)
                pe.wait_ge(xw_split, n // 2 + 1)
                pe.wait_ge(wide_read, IT_XQ + n - 1)
                for half in range(2):
                    for k in range(KD):
                        for m, (w, h) in enumerate(((xw_hi, h_hi), (xw_hi, h_lo), (xw_lo, h_hi))):
                            mm = nc.tensor.matmul(wide[(IT_XQ + n) % 2][:, HALF * half:HALF * half + HALF],
                                                  w[:, slot, k, c0:c0 + P], h[:, k, HALF * half:HALF * half + HALF],
                                                  start=(k == 0 and m == 0), stop=(k == KD - 1 and m == 2))
                mm.then_inc(wide_full, 1)

            def x_scores(u):
                head, half = u // 2, u % 2
                item = x_item[("xs", u)]
                pe.wait_ge(wide_read, max(item - 1, IT_XQ + 8))
                for n in range(4):
                    for k in range(2):
                        mm = nc.tensor.matmul(wide[item % 2][:, 256 * n:256 * n + 256],
                                              qxT[:, 2 * head + k, P * (4 * half + n):P * (4 * half + n) + P],
                                              kmT[:, 2 * head + k, :], start=(k == 0), stop=(k == 1))
                mm.then_inc(wide_full, 1)

            def x_values(u):
                head = u // 2
                item = x_item[("xo", u)]
                pe.wait_ge(xprobs_ready, u + 1)
                for m in range(2):
                    c = CH_X + 2 * u + m
                    transposes(c, [(ptb[c % 2][:, P * n:P * n + P], xprobs[:, u % 2, n, P * m:P * m + P])
                                   for n in range(4)])
                pe.wait_ge(pt_copied, CH_X + 2 * u + 2)
                pe.wait_ge(wide_read, item - 1)
                for a in range(2):
                    for m in range(2):
                        c = 256 * head + P * a
                        mm = nc.tensor.matmul(wide[item % 2][:, HALF * a:HALF * a + HALF], vm[:, m, c:c + P],
                                              xprobsT[:, u % 2, m, :], start=(m == 0), stop=(m == 1))
                mm.then_inc(wide_full, 1)

            for what, u in X_ORDER:
                (x_scores if what == "xs" else x_values)(u)
            pe.wait_ge(bigw_loaded, 32)
            pe.wait_ge(wide_read, IT_X + 16)
            for t in range(NT):
                if t >= 2:
                    pe.wait_ge(mix_read, NT + t - 1)
                for c in range(2):
                    dst = wide[t % 2][:, HALF * c:HALF * c + HALF]
                    for k in range(XO_SPLIT, KD):
                        nc.tensor.matmul(dst, o_raw[:, k, P * t:P * t + P], xo_raw[:, k, HALF * c:HALF * c + HALF],
                                         start=(k == XO_SPLIT), stop=False)
                    if t == 0 and c == 0:
                        pe.wait_ge(o_split, 6)
                        pe.wait_ge(xo_split, XO_SPLIT)
                    for k in range(XO_SPLIT):
                        for m, (o, w) in enumerate(((o_hi, xo_hi), (o_hi, xo_lo), (o_lo, xo_hi))):
                            mm = nc.tensor.matmul(dst, o[:, k, P * t:P * t + P], w[:, k, HALF * c:HALF * c + HALF],
                                                  start=False, stop=(k == XO_SPLIT - 1 and m == 2))
                mm.then_inc(mix_full, 1)
            ln_transposes("2", 0, 2 * NT + 4)

            pe.wait_ge(pt_copied, CH_LN["2", 0] + KD)
            pe.wait_ge(mix_read, 2 * NT - 1 + IT_ROUTE % 2)
            pe.wait_ge(rw_loaded, 32)
            transposed_projection(wide[IT_ROUTE % 2], rw, 0, N_EXP, halves=(0,))
            ln_transposes("2", 1, 2 * NT + 8)
            pe.wait_ge(pt_copied, CH_LN["2", 1] + KD)
            transposed_projection(wide[IT_ROUTE % 2], rw, 0, N_EXP, halves=(1,)).then_inc(wide_full, 1)
            pe.wait_ge(mix_read, 2 * NT)
            for n in range(4):
                what = ("sg", "su")[n % 2], n // 2
                w = weights(what)
                pe.wait_ge(wide_read, IT_SH + n - 1)
                transposed_projection(wide[(IT_SH + n) % 2], w, P * what[1]).then_inc(wide_full, 1)
                if n == 0:
                    pe.wait_ge(wide_read, IT_ROUTE + 1)
                    c = CH_ROUTE
                    transposes(c, [(ptb[c % 2][:, N_EXP * t:N_EXP * t + N_EXP], logitsT[:, P * t:P * t + P])
                                   for t in range(NT)])
            pe.wait_ge(routed, 1)
            pe.wait_ge(consts_ready, 7)
            sel = rs_selb.rearrange("p t e -> p (t e)")
            nc.tensor.matmul(obank, tri_b[:, :], sel, start=True, stop=True).then_inc(rank_full, 1)
            nc.tensor.matmul(sbank, ones_b[:, :], sel, start=True, stop=True).then_inc(rank_full, 1)
            last = len(w_loads) - 1
            pe.wait_ge(w_loaded[last % N_W], w_count[last])
            wd_sh = w_ring[:, last % N_W, 0:2 * D].rearrange("p (k c) -> p k c", k=2)
            pe.wait_ge(hs_ready, 2)
            pe.wait_ge(wide_read, IT_SH + 4)
            for t in range(NT):
                if t == 5:
                    pe.wait_ge(blk_full, 1)
                    nc.tensor.transpose(obank[0:1, 0:P], blk_exp[:, 0:1], ident[:, :])
                    nc.tensor.transpose(obank[0:1, P:2 * P], blk_exp[:, 1:2], ident[:, :]).then_inc(rank_full, 1)
                if t >= 2:
                    pe.wait_ge(mix_read, 2 * NT + t - 1)
                for c in range(2):
                    for k in range(2):
                        mm = nc.tensor.matmul(wide[t % 2][:, HALF * c:HALF * c + HALF],
                                              hs[:, k, P * t:P * t + P], wd_sh[:, k, HALF * c:HALF * c + HALF],
                                              start=(k == 0), stop=(k == 1))
                mm.then_inc(mix_full, 1)


            def frames_of_block(b, count, read):
                pe.wait_ge(onehot_ready, count)
                if read is not None:
                    pe.wait_ge(idx_ready, read)
                for t in range(NT):
                    mm = nc.tensor.matmul(sbank[:, 8 * b:8 * b + 6], onehot[:, b, t, :], slot_cols[:, b, t, :],
                                          start=(t == 0), stop=(t == NT - 1))
                mm.then_inc(idx_full, 1)

            def rows_transposed(b, landed, free):
                pe.wait_ge(gathered[b], landed)
                for n in range(2):
                    if free is not None:
                        pe.wait_ge(xt_copied, free + n)
                    for a in range(4):
                        k = 4 * n + a
                        mm = nc.tensor.transpose(ptb[n][:, P * a:P * a + P], xg[:, b, P * k:P * k + P],
                                                 ident[:, :])
                    mm.then_inc(xt_full, 1)

            pe.wait_ge(table_ready, 1)
            pe.wait_ge(pt_copied, CH_MOE)
            pe.wait_ge(mix_read, 3 * NT)
            for j in range(2):
                frames_of_block(j, j + 1, j or None)
            rows_transposed(0, 16, None)
            turns = pe.value_load(table[0:1, TURNS:TURNS + 1], min_val=1, max_val=MAX_TURNS)
            with pe.Fori(0, turns) as i:
                for b in range(2):
                    pe.wait_ge(xt_copied, 4 * i + 2 * b + 2)
                    pe.wait_ge(gu_split, 2 * GU_PARTS * i + GU_PARTS * b + GU_PARTS)
                    for k in range(KD):
                        for n, (x, w) in enumerate(((xgT_hi, gu_hi), (xgT_hi, gu_lo), (xgT_lo, gu_hi))):
                            mm = nc.tensor.matmul(wide[0][:, HALF * b:HALF * b + HALF], x[:, b, k, :],
                                                  w[b][:, k, :], start=(k == 0 and n == 0),
                                                  stop=(k == KD - 1 and n == 2))
                    mm.then_inc(gu_full, 1)
                    frames_of_block(b, 2 * i + b + 3, 2 * i + b + 2)
                    rows_transposed(1 - b, 16 * i + 16 + 16 * b, 4 * i + 2 * b + 1)
                    pe.wait_ge(h_ready, 2 * i + b + 1)
                    for k in range(2):
                        mm = nc.tensor.transpose(obank[:, 256 * b + P * k:256 * b + P * k + P],
                                                 h_exp[:, b, P * k:P * k + P], ident[:, :])
                    mm.then_inc(ht_full, 1)
                    pe.wait_ge(ht_copied, 2 * i + b + 1)
                    pe.wait_ge(wd_loaded[b], 16 * i + 16)
                    pe.wait_ge(y_ready, 2 * i + b + 1)
                    for c in range(2):
                        for k in range(2):
                            mm = nc.tensor.matmul(wide[1][:, HALF * c:HALF * c + HALF], hT_exp[:, b, k, :],
                                                  wd_w[b][:, k, HALF * c:HALF * c + HALF],
                                                  start=(k == 0), stop=(k == 1))
                    mm.then_inc(y_full, 1)

        @block.scalar
        def _(act):
            def chunk_full(c):
                act.wait_ge(pt_full, c + 1)

            def ln_root(ln, t):
                act.wait_ge(ln_stat, NT * ln + t + 1)
                nc.scalar.activation(rstd[:, t:t + 1], mv[:, t, 1:2], ACT.Sqrt, bias=LN_EPS).then_inc(ln_std, 1)

            def ln_copy(which, half, k):
                c = CH_LN[which, half] + k
                r = R_LN[which]
                chunk_full(c)
                dst = h_raw if which == "1" else hT
                nc.scalar.activation(dst[:, k, HALF * half:HALF * half + HALF], ptb[c % 2], ACT.Identity,
                                     bias=cols[:, r[1] + k:r[1] + k + 1],
                                     scale=cols[:, r[0] + k:r[0] + k + 1]).then_inc(pt_copied, 1)

            for t in range(3):
                ln_root(0, t)
            chunk_full(0)
            nc.scalar.copy(cols[:, :], ptb[0][:, 0:N_ROWS]).then_inc(pt_copied, 1)
            act.wait_ge(pt_copied, 1)
            ln_root(0, 3)
            for k in range(KD):
                ln_copy("in", 0, k)
                if k % 2:
                    ln_root(0, 4 + k // 2)
            for k in range(KD):
                ln_copy("in", 1, k)

            def item_full(item):
                act.wait_ge(wide_full, item + 1)

            def projected(what):
                item = item_of[what]
                item_full(item)
                src = wide[item % 2]
                kind, n = what[0], what[1]
                group = {0: 0, 1: 1, 2: 2, 3: 2, 4: 3, 5: 4}[n]
                slot = SLOT_OF[group]
                if kind == "a":
                    last = nc.scalar.copy(z[:, n, PAD:PAD + S], src)
                elif kind == "g":
                    last = nc.scalar.activation(sig[:, n, :], src, ACT.Sigmoid)
                elif kind == "q":
                    act.wait_ge(q_zeroed, Q_ZEROED[group])
                    if group < 2:
                        for m in range(4):
                            last = nc.scalar.mul(Q[slot][32 * m:32 * m + 32, m, :], src[32 * m:32 * m + 32, :],
                                                 32 ** -0.5)
                    else:
                        for p in range(2):
                            m = p if group > 2 else (n - 2) + 2 * p
                            last = nc.scalar.mul(Q[slot][64 * p:64 * p + 64, m, :], src[64 * p:64 * p + 64, :],
                                                 0.125)
                elif kind == "k" and group > 2:
                    for p in range(2):
                        last = nc.scalar.copy(K[slot][64 * p:64 * p + 64, p, :], src[64 * p:64 * p + 64, :])
                elif kind == "k":
                    last = nc.scalar.copy(K[slot][:, 0, :], src)
                elif n == 0:
                    last = nc.scalar.copy(V[0][:, 4 * what[2]:4 * what[2] + 4, :],
                                          src.rearrange("p (t c) -> p t c", t=4))
                elif n == 2:
                    last = nc.scalar.copy(V[1][:, :, 0:P], src.rearrange("p (t c) -> p t c", t=NT))
                else:
                    two = src.rearrange("p (t c) -> p t c", t=2)
                    t = 2 * what[2]
                    act.wait_ge(pv_done, DIFF_STEPS)
                    nc.scalar.copy(logf[:, 0, t:t + 2, :], two[:, :, 256:260])
                    last = nc.scalar.copy(V[0][:, t:t + 2, :], two[:, :, 0:256])
                last.then_inc(wide_read, 1)

            def exponentials(s):
                group, kind, pair, parity, tile = STEPS[s]
                n = P * len(key_tiles(kind, tile))
                if s == 0:
                    act.wait_ge(glu_done, 2)
                if s >= 2:
                    act.wait_ge(pt_full, chunk_of[s - 1])
                for m in range(2 if kind == "diff" else 1):
                    item = item_of[("s", s, m)]
                    act.wait_ge(row_max, RMS_OF[(s, m)] + 1)
                    bias = negm[:, s % 2, m:m + 1]
                    if kind == "swa":
                        h = 2 * pair + parity
                        nc.scalar.activation(sums[:, s % 2, 1:2], sink[:, h:h + 1], ACT.Exp, bias=bias)
                    nc.scalar.activation(probs[:, s % 2, m, 0:n], wide[item % 2][:, 0:n], ACT.Exp, bias=bias,
                                         accum_out=sums[:, s % 2, m:m + 1]).then_inc(wide_read, 1)
                if s == FOX_LOG_AT:
                    act.wait_ge(fox_z, 1)
                    nc.scalar.activation(logf[:, 1], logf[:, 1], ACT.Exp).then_inc(fox_e, 1)
                    act.wait_ge(fox_e, 1)
                    nc.scalar.activation(logf[:, 1], logf[:, 1], ACT.Ln, bias=1.0).then_inc(fox_l, 1)

            def transposed(s):
                kind, tile = STEPS[s][1], STEPS[s][4]
                keys = key_tiles(kind, tile)
                if s == 0:
                    for n in range(2):
                        act.wait_ge(res_stored[n], 64)
                if s >= 2:
                    act.wait_ge(pv_done, s - 1)
                for n in range((len(keys) + 3) // 4):
                    c, b = chunk_of[s] + n, min(4, len(keys) - 4 * n)
                    chunk_full(c)
                    nc.scalar.copy(probsT[:, s % 2, 4 * n:4 * n + b, :],
                                   ptb[c % 2][:, 0:P * b].rearrange("p (k q) -> p k q", k=b)
                                   ).then_inc(pt_copied, 1)

            act.wait_ge(lam_sum, 1)
            nc.scalar.activation(lam[:, 2:4], lam[:, 0:2], ACT.Exp).then_inc(lam_exp, 1)
            for kind, what in PLAN:
                if kind == "proj":
                    projected(what)
                elif kind == "cum":
                    item_full(item_of[what])
                    nc.scalar.copy(cumT, wide[item_of[what] % 2]).then_inc(wide_read, 1)
                elif kind == "scores":
                    exponentials(what)
                elif kind == "turn":
                    transposed(what)

            act.wait_ge(o_read, NS // 2)
            for c in range(2):
                nc.scalar.activation(squares[:, c, :], yT[:, c, :], ACT.Square).then_inc(sq_ready, 1)
            for h in range(2):
                act.wait_ge(cln_stat, 4 * h + 4)
                nc.scalar.activation(rstd[:, 4 * h:4 * h + 4], mv[:, 4 * h:4 * h + 4, 1], ACT.Sqrt,
                                     bias=LN_EPS).then_inc(cln_std, 1)
            for c in range(2):
                act.wait_ge(rms_full, c + 1)
                nc.scalar.activation(root[:, c, :], rms_psum[c], ACT.Ln, bias=LN_EPS).then_inc(rms_log, 1)
            for c in range(2):
                act.wait_ge(rms_log, c + 1)
                nc.scalar.activation(root[:, c, :], root[:, c, :], ACT.Exp, scale=-0.5).then_inc(rms_root, 1)
            for h in range(2):
                act.wait_ge(cln_back, h + 1)
                for c in range(2):
                    last = nc.scalar.activation(yT[:, 2 + c, HALF * h:HALF * h + HALF],
                                                wide[h][:, HALF * c:HALF * c + HALF], ACT.Silu,
                                                bias=cols[:, R_CLNB + c:R_CLNB + c + 1],
                                                scale=cols[:, R_CLNG + c:R_CLNG + c + 1])
                last.then_inc(cln_act, 1)
            for t in range(5):
                ln_root(1, t)
            for k in range(KD):
                ln_copy("1", 0, k)
            for t in range(5, NT):
                ln_root(1, t)
            for n in range(4):
                c = CH_MEM + n
                chunk_full(c)
                nc.scalar.copy(memT[:, 2 * n:2 * n + 2, :], ptb[c % 2].rearrange("p (k m) -> p k m", k=2)
                               ).then_inc(pt_copied, 1)
            def round_query_weights(n):
                load = XQ_LOAD + n
                act.wait_ge(w_loaded[load % N_W], w_count[load])
                nc.scalar.copy(xw_hi[:, n % 2], xw_raw[:, load % N_W, 0:2 * U].rearrange("p (k c) -> p k c", k=KD)
                               ).then_inc(xw_rounded, 1)

            for n in range(4):
                if n == 3:
                    round_query_weights(0)
                item_full(IT_MEM + n)
                src = wide[(IT_MEM + n) % 2]
                if n < 2:
                    last = nc.scalar.copy(kmT[:, 4 * n:4 * n + 4, :], src.rearrange("p (k m) -> p k m", k=4))
                else:
                    four = src.rearrange("p (r a c) -> p r a c", r=2, a=2)
                    for a in range(2):
                        last = nc.scalar.copy(vm[:, a, HALF * (n - 2):HALF * (n - 1)]
                                              .rearrange("p (r c) -> p r c", r=2), four[:, :, a, :])
                last.then_inc(wide_read, 1)
                if n == 0:
                    for k in range(KD):
                        ln_copy("1", 1, k)

            round_query_weights(1)
            act.wait_ge(res_ready, 2 * NT)
            for n in range(8):
                item_full(IT_XQ + n)
                nc.scalar.mul(qxT[:, n, :], wide[(IT_XQ + n) % 2], 1.0 / 16).then_inc(wide_read, 1)
                if n in (1, 3):
                    round_query_weights(2 + n // 2)
            def x_transposed(u):
                if u == 0:
                    for n in range(2):
                        act.wait_ge(res_stored[n], 128)
                for m in range(2):
                    c = CH_X + 2 * u + m
                    chunk_full(c)
                    nc.scalar.copy(xprobsT[:, u % 2, m, :], ptb[c % 2]).then_inc(pt_copied, 1)

            for what, u in X_ORDER:
                item = x_item[(what, u)]
                src = wide[item % 2]
                if what == "xs":
                    if u:
                        x_transposed(u - 1)
                    act.wait_ge(xmax, u + 1)
                    if u >= 2:
                        act.wait_ge(pt_full, CH_X + 2 * u - 2)
                    for n in range(4):
                        last = nc.scalar.activation(xprobs[:, u % 2, n, :], src[:, 256 * n:256 * n + 256], ACT.Exp,
                                                    bias=xneg[:, u % 2, n:n + 1],
                                                    accum_out=xsum[:, u % 2, n:n + 1])
                    last.then_inc(wide_read, 1)
                else:
                    if u == 7:
                        x_transposed(7)
                    item_full(item)
                    k, half = 2 * (u // 2), u % 2
                    frames_h = slice(HALF * half, HALF * half + HALF)
                    nc.scalar.copy(o_raw[:, k:k + 2, frames_h],
                                   src.rearrange("p (a s) -> p a s", a=2)).then_inc(wide_read, 1)
                    if k < XO_SPLIT:
                        act.wait_ge(wide_read, item + 1)
                        nc.scalar.copy(o_hi[:, k:k + 2, frames_h], o_raw[:, k:k + 2, frames_h]).then_inc(o_rounded, 1)
                    if 1 <= u <= XO_SPLIT:
                        if u == 1:
                            act.wait_ge(bigw_loaded, 32)
                        nc.scalar.copy(xo_hi[:, u - 1, :], xo_raw[:, u - 1, :]).then_inc(xo_rounded, 1)
            for t in range(5):
                ln_root(2, t)
            for k in range(KD):
                ln_copy("2", 0, k)
            for t in range(5, NT):
                ln_root(2, t)
            for k in range(KD):
                ln_copy("2", 1, k)
            item_full(IT_ROUTE)
            nc.scalar.copy(logitsT, wide[IT_ROUTE % 2][0:N_EXP, :]).then_inc(wide_read, 1)
            chunk_full(CH_ROUTE)
            nc.scalar.activation(rs_scores, ptb[CH_ROUTE % 2].rearrange("p (t e) -> p t e", t=NT),
                                 ACT.Sigmoid).then_inc(pt_copied, 1)
            for m in range(2):
                item_full(IT_SH + 2 * m)
                nc.scalar.activation(hs[:, m, :], wide[(IT_SH + 2 * m) % 2], ACT.Silu).then_inc(wide_read, 1)
                item_full(IT_SH + 2 * m + 1)
                if m:
                    act.wait_ge(hs_ready, 1)
                nc.scalar.copy(hs_tmp, wide[(IT_SH + 2 * m + 1) % 2]).then_inc(wide_read, 1)

            acc_dram = acc.rearrange("(t p) d -> t p d", p=P)
            for t in range(NT):
                act.wait_ge(mix_read, 2 * NT + t + 1)
                act.dma_start(acc_dram[t], xnorm["2"][:, t, :]).then_inc(acc_stored, 16)

            act.sem_inc(y_ready, 1)
            def copy_rows(b, n, full):
                act.wait_ge(xt_full, full)
                nc.scalar.copy(xgT_hi[:, b, 4 * n:4 * n + 4, :],
                               ptb[n].rearrange("p (k r) -> p k r", k=4)).then_inc(xt_rounded, 1)

            def round_weights(b, parts):
                for q in parts:
                    nc.scalar.copy(gu_hi[b][:, 2 * q:2 * q + 2, :],
                                   gu_w[b][:, 2 * q:2 * q + 2, :]).then_inc(gu_rounded, 1)

            act.wait_ge(mix_full, 3 * NT)
            act.wait_ge(gu_loaded[0], 32)
            round_weights(0, range(GU_PARTS))
            for n in range(2):
                copy_rows(0, n, n + 1)
            act.wait_ge(table_ready, 1)
            turns = act.value_load(table[0:1, TURNS:TURNS + 1], min_val=1, max_val=MAX_TURNS)
            with act.Fori(0, turns) as i:
                for b in range(2):
                    act.wait_ge(gu_loaded[1 - b], 32 * i + 32 + 32 * b)
                    round_weights(1 - b, range(0, A_SPLIT))
                    act.wait_ge(gu_full, 2 * i + b + 1)
                    nc.scalar.activation(h_exp[:, b, :], wide[0][:, HALF * b:HALF * b + D_EXP],
                                         ACT.Silu).then_inc(silu_done, 1)
                    for n in range(2):
                        copy_rows(1 - b, n, 4 * i + 2 * b + n + 3)
                    round_weights(1 - b, range(A_SPLIT, GU_PARTS))
                    act.wait_ge(y_full, 2 * i + b + 1)
                    act.wait_ge(scattered, 32 * i + 16 * b + 16)
                    nc.scalar.copy(y_exp[:, b, :], wide[1]).then_inc(y_ready, 1)
            for t in range(NT + 1):
                if t < NT:
                    ln_root(3, t)
                if t:
                    u = t - 1
                    act.wait_ge(out_scale, u + 1)
                    nc.scalar.activation(xnorm["3"][:, u, :], xnorm["3"][:, u, :], ACT.Identity,
                                         bias=nbias[:, u:u + 1], scale=rstd[:, u:u + 1]).then_inc(out_norm, 1)

        @block.vector
        def _(dve):
            chain = [0]

            def link(made):
                chain[0] += 1
                made.then_inc(dve_step, 1)
                dve.wait_ge(dve_step, chain[0])

            def layer_norm_tiles(ln, tile_ready):
                x = xnorm["in" if ln == 0 else str(ln)]
                for t in range(NT + 1):
                    if t < NT:
                        tile_ready(t)
                        for h in range(2):
                            last = nc.vector.bn_stats(stats[:, t, h, :], x[:, t, HALF * h:HALF * h + HALF])
                        link(last)
                        nc.vector.bn_aggr(mv[:, t, :], stats[:, t, :, :]).then_inc(ln_stat, 1)
                    if t:
                        u = t - 1
                        dve.wait_ge(ln_std, NT * ln + u + 1)
                        link(nc.vector.reciprocal(rstd[:, u:u + 1], rstd[:, u:u + 1]))
                        nc.vector.tensor_scalar(x[:, u, :], x[:, u, :], mv[:, u, 0:1], rstd[:, u:u + 1],
                                                ALU.subtract, ALU.mult).then_inc(ln_done, 1)

            layer_norm_tiles(0, lambda t: dve.wait_ge(x_loaded[t], 16))
            dve.wait_ge(params_loaded, 96)
            for n in range(2):
                last = nc.vector.tensor_tensor_reduce(lamv[:, 2 * n, :], lamv[:, 2 * n, :], lamv[:, 2 * n + 1, :],
                                                      1.0, 0.0, ALU.mult, ALU.add, lam[:, n:n + 1])
            last.then_inc(lam_sum, 1)
            dve.wait_ge(lam_exp, 1)
            link(nc.vector.tensor_tensor(lam[:, 4:5], lam[:, 3:4], lam[:, 2:3], ALU.subtract))
            link(nc.vector.tensor_scalar(lam[:, 5:6], lam[:, 4:5], -LAMBDA_INIT, None, ALU.add))
            neg_lam = lam[:, 5:6]
            nc.vector.tensor_scalar(nsink[:, :], sink[:, :], -1.0, None, ALU.mult)
            dve.wait_ge(pt_copied, 1)
            link(nc.vector.tensor_scalar(subg[:, :], cols[:, R_SUBG:R_SUBG + 1], 1.0 - LAMBDA_INIT, None, ALU.mult))
            def conv_tap(n):
                c, k = n // CONV_K, n % CONV_K
                w = cols[:, R_CONVW + n:R_CONVW + n + 1]
                if k == 0:
                    dve.wait_ge(glu_done, c + 1)
                    nc.vector.tensor_scalar(zc[:, c, :], z[:, c, 0:S], w, cols[:, R_CONVB + c:R_CONVB + c + 1],
                                            ALU.mult, ALU.add).then_inc(conv_done, 1)
                else:
                    dve.wait_ge(conv_done, n)
                    nc.vector.scalar_tensor_tensor(zc[:, c, :], z[:, c, k:k + S], w, zc[:, c, :],
                                                   ALU.mult, ALU.add).then_inc(conv_done, 1)

            for c in range(2):
                link(nc.vector.memset(z[:, c, 0:PAD], 0.0))
                dve.wait_ge(wide_read, item_of[("g", c)] + 1)
                nc.vector.tensor_tensor(z[:, c, PAD:PAD + S], z[:, c, PAD:PAD + S], sig[:, c, :],
                                        ALU.mult).then_inc(glu_done, 1)
                for n in range(CONV_K * c, CONV_K * c + CONV_K):
                    conv_tap(n)

            def maxima(s):
                group, kind, pair, parity, tile = STEPS[s]
                n = P * len(key_tiles(kind, tile))
                for m in range(2 if kind == "diff" else 1):
                    item = item_of[("s", s, m)]
                    dve.wait_ge(wide_full, item + 1)
                    made = nc.vector.tensor_reduce(negm[:, s % 2, m:m + 1], wide[item % 2][:, 0:n], AX.X, ALU.max,
                                                   negate=True)
                    if kind == "swa":
                        h = 2 * pair + parity
                        link(made)
                        made = nc.vector.tensor_tensor(negm[:, s % 2, 0:1], negm[:, s % 2, 0:1],
                                                       nsink[:, h:h + 1], ALU.min)
                    made.then_inc(row_max, 1)

            def normalise(s):
                kind, tile = STEPS[s][1], STEPS[s][4]
                n = P * len(key_tiles(kind, tile))
                maps = 2 if kind == "diff" else 1
                p = probs[:, s % 2]
                r = rsum[:, s % 2]
                dve.wait_ge(wide_read, item_of[("s", s, maps - 1)] + 1)
                if kind == "diff":
                    link(nc.vector.reciprocal(r[:, 0:2], sums[:, s % 2, :]))
                    link(nc.vector.tensor_tensor(r[:, 2:3], r[:, 1:2], neg_lam, ALU.mult))
                    link(nc.vector.tensor_scalar(p[:, 1, 0:n], p[:, 1, 0:n], r[:, 2:3], None, ALU.mult))
                    nc.vector.scalar_tensor_tensor(p[:, 0, 0:n], p[:, 0, 0:n], r[:, 0:1], p[:, 1, 0:n],
                                                   ALU.mult, ALU.add).then_inc(probs_ready, 1)
                    return
                total = sums[:, s % 2, 0:1]
                if kind == "swa":
                    link(nc.vector.tensor_tensor(r[:, 1:2], sums[:, s % 2, 0:1], sums[:, s % 2, 1:2], ALU.add))
                    total = r[:, 1:2]
                link(nc.vector.reciprocal(r[:, 0:1], total))
                nc.vector.tensor_scalar(p[:, 0, 0:n], p[:, 0, 0:n], r[:, 0:1], None, ALU.mult).then_inc(probs_ready, 1)

            def augment(group):
                pair, slot = group - 3, SLOT_OF[group]
                dve.wait_ge(wide_read, item_of["cum"] + 1)
                dve.wait_ge(q_zeroed, Q_ZEROED[group])
                for p in range(2):
                    row, at0 = 32 * (2 * pair + p), (64, 0)[p]
                    nc.vector.tensor_copy(Q[slot][at0:at0 + 1, p, :], cumT[row:row + 1, :])
                    last = nc.vector.tensor_scalar(K[slot][at0 + 32:at0 + 33, p, :], cumT[row:row + 1, :],
                                                   -1.0, None, ALU.mult)
                last.then_inc(aug_ready, 1)

            def output_read(pair_step):
                s = 2 * pair_step
                _, kind, pair, _, tile = STEPS[s]
                dve.wait_ge(pv_done, s + 2)
                nc.vector.tensor_copy(yT[:, Y_CHUNK[kind] + pair, P * tile:P * tile + P],
                                      (obank, sbank)[pair_step % 2][:, 0:P]).then_inc(o_read, 1)

            def fox_log():
                x = logf[:, 0]
                link(nc.vector.tensor_tensor(x, x, foxb[:, :].unsqueeze(1).broadcast_to([P, NT, 4]), ALU.add))
                nc.vector.scalar_tensor_tensor(logf[:, 1], x, -1.0, x, ALU.mult, ALU.min).then_inc(fox_z, 1)
                dve.wait_ge(res_ready, NT)
                link(nc.vector.memset(fstat, 0.0))

            def fox_log_end():
                dve.wait_ge(fox_l, 1)
                nc.vector.scalar_tensor_tensor(fstat[:, :, 0:P:32], logf[:, 0], 0.0, logf[:, 1],
                                               ALU.min, ALU.subtract).then_inc(fstat_ready, 1)

            for kind, what in PLAN:
                if kind == "scores":
                    if what == FOX_LOG_AT:
                        fox_log()
                    if what:
                        normalise(what - 1)
                    maxima(what)
                    if what == FOX_LOG_AT + 1:
                        fox_log_end()
                    if what in AUGMENT_AT:
                        augment(3 + AUGMENT_AT.index(what))
                elif kind == "turn" and what == NS - 1:
                    normalise(what)
                elif kind == "values":
                    if what % 2 == 0 and what >= 2:
                        output_read(what // 2 - 1)
            output_read(NS // 2 - 1)

            dve.wait_ge(pt_full, ATT_CHUNKS)
            link(nc.vector.memset(blk_ones, 0.0))
            for p in range(2):
                last = nc.vector.memset(blk_ones[64 * p:64 * p + 64, 64 * p:64 * p + 64], 1.0 / 64)
            last.then_inc(blk_ready, 1)
            for h in range(2):
                dve.wait_ge(cln_full, h + 1)
                for n in range(4):
                    last = nc.vector.bn_stats(stats[:, 4 * h + n, 0, :], wide[h][:, 256 * n:256 * n + 256])
                link(last)
                for n in range(4):
                    nc.vector.bn_aggr(mv[:, 4 * h + n, :], stats[:, 4 * h + n, 0, :]).then_inc(cln_stat, 1)
            for h in range(2):
                dve.wait_ge(cln_std, h + 1)
                link(nc.vector.reciprocal(rstd[:, 4 * h:4 * h + 4], rstd[:, 4 * h:4 * h + 4]))
                for n in range(4):
                    t = 4 * h + n
                    last = nc.vector.tensor_scalar(cln_x[:, h, n, :], wide[h][:, 256 * n:256 * n + 256],
                                                   mv[:, t, 0:1], rstd[:, t:t + 1], ALU.subtract, ALU.mult)
                last.then_inc(cln_xn, 1)
            for c in range(2):
                dve.wait_ge(rms_root, c + 1)
                nc.vector.scalar_tensor_tensor(yT[:, c, :], yT[:, c, :], subg[:, 0:1], root[:, c, :],
                                               ALU.mult, ALU.mult).then_inc(rms_done, 1)

            def add_products(ln, first):
                def ready(t):
                    n = first + t
                    dve.wait_ge(x_loaded[t], 16 * (ln + 1))
                    dve.wait_ge(mix_full, n + 1)
                    x = xnorm[str(ln)][:, t, :]
                    nc.vector.tensor_tensor(x, x, wide[t % 2], ALU.add).then_inc(mix_read, 1)
                    dve.wait_ge(mix_read, n + 1)
                return ready

            layer_norm_tiles(1, add_products(1, 0))
            for half in range(2):
                for k in range(KD):
                    cols_h = slice(HALF * half, HALF * half + HALF)
                    dve.wait_ge(pt_copied, CH_LN["1", half] + k + 1)
                    link(nc.vector.tensor_copy(h_hi[:, k, cols_h], h_raw[:, k, cols_h]))
                    nc.vector.tensor_tensor(h_lo[:, k, cols_h], h_raw[:, k, cols_h],
                                            h_hi[:, k, cols_h].bitcast(F32), ALU.subtract).then_inc(h_split, 1)
            for n in range(4):
                load = XQ_LOAD + n
                dve.wait_ge(xw_rounded, n + 1)
                nc.vector.tensor_tensor(xw_lo[:, n % 2],
                                        xw_raw[:, load % N_W, 0:2 * U].rearrange("p (k c) -> p k c", k=KD),
                                        xw_hi[:, n % 2].bitcast(F32), ALU.subtract).then_inc(xw_split, 1)
            for u in range(8):
                item = x_item[("xs", u)]
                dve.wait_ge(wide_full, item + 1)
                nc.vector.tensor_reduce(xneg[:, u % 2, :], wide[item % 2].rearrange("p (t m) -> p t m", t=4), AX.X,
                                        ALU.max, negate=True).then_inc(xmax, 1)
                dve.wait_ge(wide_read, item + 1)
                link(nc.vector.reciprocal(xsum[:, u % 2, :], xsum[:, u % 2, :]))
                nc.vector.tensor_tensor(xprobs[:, u % 2], xprobs[:, u % 2],
                                        xsum[:, u % 2, :].unsqueeze(2).broadcast_to([P, 4, N_MEM]),
                                        ALU.mult).then_inc(xprobs_ready, 1)
                if u >= 2:
                    k, frames_h = 2 * ((u - 2) // 2), slice(HALF * (u % 2), HALF * (u % 2) + HALF)
                    dve.wait_ge(o_rounded, u - 1)
                    nc.vector.tensor_tensor(o_lo[:, k:k + 2, frames_h], o_raw[:, k:k + 2, frames_h],
                                            o_hi[:, k:k + 2, frames_h].bitcast(F32),
                                            ALU.subtract).then_inc(o_split, 1)
                for k in ((u - 3,) if 3 <= u < 7 else (4, 5) if u == 7 else ()):
                    dve.wait_ge(xo_rounded, k + 1)
                    nc.vector.tensor_tensor(xo_lo[:, k, :], xo_raw[:, k, :], xo_hi[:, k, :].bitcast(F32),
                                            ALU.subtract).then_inc(xo_split, 1)
            layer_norm_tiles(2, add_products(2, NT))

            def hidden(m):
                dve.wait_ge(wide_read, IT_SH + 2 * m + 2)
                nc.vector.tensor_tensor(hs[:, m, :], hs[:, m, :], hs_tmp, ALU.mult).then_inc(hs_ready, 1)

            dve.wait_ge(pt_copied, CH_ROUTE + 1)
            nc.vector.memset(rs_choice[:, :, N_EXP:N_EXP + 2], SENTINEL)
            nc.vector.memset(gsum[:, :, N_GRP:12], SENTINEL)
            link(nc.vector.tensor_tensor(rs_choice[:, :, 0:N_EXP], rs_scores,
                                         rbias.unsqueeze(1).broadcast_to([P, NT, N_EXP]), ALU.add))
            for t in range(NT):
                for g in range(N_GRP):
                    last = nc.vector.max(top8[:, t, g, :], rs_choice[:, t, PER_GRP * g:PER_GRP * g + PER_GRP])
            link(last)
            link(nc.vector.tensor_tensor(gsum[:, :, 0:N_GRP], top8[:, :, :, 0], top8[:, :, :, 1], ALU.add))

            def take_top(n_take, values, n_values, n_padded, largest):
                for t in range(NT):
                    last = nc.vector.max(largest[:, t, :], values[:, t, 0:n_values])
                link(last)
                link(nc.vector.memset(largest[:, :, n_take:8], SENTINEL))
                for t in range(NT):
                    last = nc.vector.match_replace(values[:, t, 0:n_padded], largest[:, t, :],
                                                   values[:, t, 0:n_padded], TAKEN)
                link(last)

            take_top(TOP_GRP, gsum, N_GRP, 12, gtop)
            link(nc.vector.tensor_scalar(gpen[:, :, 0:N_GRP], gsum[:, :, 0:N_GRP], TAKEN / 3, NEG, ALU.is_lt, ALU.mult))
            by_group = rs_choice[:, :, 0:N_EXP].rearrange("p t (g e) -> p t g e", g=N_GRP)
            for t in range(NT):
                last = nc.vector.tensor_tensor(by_group[:, t], by_group[:, t],
                                               gpen[:, t, 0:N_GRP].unsqueeze(2).broadcast_to([P, N_GRP, PER_GRP]),
                                               ALU.add)
            link(last)
            take_top(TOP_K, rs_choice, N_EXP, N_EXP + 2, gtop)
            link(nc.vector.tensor_scalar(rs_sel, rs_choice[:, :, 0:N_EXP], TAKEN / 3, None, ALU.is_gt))
            nc.vector.tensor_copy(rs_selb, rs_sel).then_inc(routed, 1)
            hidden(0)
            link(nc.vector.tensor_tensor(rs_gate, rs_sel, rs_scores, ALU.mult))
            link(nc.vector.tensor_reduce(gden[:, :, 0], rs_gate, AX.X, ALU.add))
            link(nc.vector.reciprocal(gden[:, :, 1], gden[:, :, 0]))
            link(nc.vector.tensor_tensor(rs_gate, rs_gate, gden[:, :, 1].unsqueeze(2).broadcast_to([P, NT, N_EXP]),
                                         ALU.mult))
            link(nc.vector.tensor_scalar(rs_gate, rs_gate, ROUTED_SCALE, None, ALU.mult))
            for g in range(3):
                part = gparts[:, :, :, g].rearrange("p e t -> p t e")
                link(nc.vector.tensor_copy(part, rs_gate))
                if g < 2:
                    link(nc.vector.tensor_tensor(rs_gate, rs_gate, part, ALU.subtract))
            hidden(1)
            dve.wait_ge(h_stored, 16 * NT)

            def start_sum(t):
                dve.wait_ge(mix_full, 2 * NT + t + 1)
                x = xnorm["2"][:, t, :]
                nc.vector.scalar_tensor_tensor(x, x, ALPHA, wide[t % 2], ALU.mult, ALU.add).then_inc(mix_read, 1)

            dve.wait_ge(rank_full, 2)
            counts = sbank.rearrange("p (t e) -> p t e", t=NT)
            link(nc.vector.memset(rs_off[:, 0, :], 0.0))
            for t in range(NT):
                link(nc.vector.tensor_tensor(rs_off[:, t + 1, :], rs_off[:, t, :], counts[:, t, :], ALU.add))
            link(nc.vector.tensor_tensor(rs_rank, rs_off[:, 0:NT, :], obank.rearrange("p (t e) -> p t e", t=NT),
                                         ALU.add))
            start_sum(0)
            link(nc.vector.tensor_scalar(nb_i[:, :], rs_off[:, NT, :], float(EXP_BLOCK - 1), None, ALU.add))
            link(nc.vector.tensor_scalar(nb_i[:, :], nb_i[:, :], 7, None, ALU.logical_shift_right))
            link(nc.vector.tensor_copy(nb_f[:, 0, :], nb_i[:, :]))
            link(nc.vector.tensor_copy(nb_f[:, 1, :], nb_f[:, 0, :]))
            src, k = 1, 1
            while k < N_EXP:
                dst = 3 - src
                nc.vector.tensor_copy(nb_f[:, dst, 0:k], nb_f[:, src, 0:k])
                link(nc.vector.tensor_tensor(nb_f[:, dst, k:], nb_f[:, src, k:], nb_f[:, src, 0:N_EXP - k], ALU.add))
                src, k = dst, 2 * k
                if k in (8, N_EXP):
                    start_sum(1 if k == 8 else 2)
            ends = nb_f[:, src, :]
            starts = nb_f[:, 0, :]
            tmp = nb_f[:, 3 - src, :]
            link(nc.vector.tensor_scalar(turn_i[:, :], ends[:, N_EXP - 1:N_EXP], 1.0, None, ALU.add))
            link(nc.vector.tensor_scalar(turn_i[:, :], turn_i[:, :], 1, None, ALU.logical_shift_right))
            nc.vector.tensor_copy(table[0:1, TURNS:TURNS + 1], turn_i[0:1, :])
            nc.vector.memset(blk_base[:, 0:1], 0.0)
            link(nc.vector.tensor_copy(blk_base[:, 1:2], turn_i[:, :]))
            nc.vector.tensor_tensor(pcol[:, 3:4], pcol[:, 0:1], blk_base[:, 1:2], ALU.add)
            link(nc.vector.tensor_scalar(tmp, ends, pcol[:, 0:1], None, ALU.is_le))
            link(nc.vector.tensor_reduce(blk_exp[:, 0:1], tmp, AX.X, ALU.add))
            link(nc.vector.tensor_scalar(tmp, ends, pcol[:, 3:4], None, ALU.is_le))
            link(nc.vector.tensor_reduce(blk_exp[:, 1:2], tmp, AX.X, ALU.add))
            nc.vector.tensor_scalar(blk_exp[:, :], blk_exp[:, :], float(N_EXP - 1), None,
                                    ALU.min).then_inc(blk_full, 1)
            start_sum(3)
            link(nc.vector.tensor_scalar(blk_base[:, 1:2], blk_base[:, 1:2], float(EXP_BLOCK), None, ALU.mult))
            link(nc.vector.tensor_tensor(starts, ends, starts, ALU.subtract))
            link(nc.vector.tensor_scalar(starts, starts, float(EXP_BLOCK), 1.0, ALU.mult, ALU.add))
            link(nc.vector.tensor_tensor(rs_rank, rs_rank, starts.unsqueeze(1).broadcast_to([P, NT, N_EXP]), ALU.add))
            link(nc.vector.tensor_tensor(rs_rank, rs_rank, rs_sel, ALU.mult))
            link(nc.vector.tensor_scalar(dest.rearrange("p e t -> p t e"), rs_rank, -1.0, None, ALU.add))
            start_sum(4)
            nc.vector.memset(y_exp[:, 0, :], 0.0).then_inc(moe_setup, 1)
            dve.wait_ge(rank_full, 3)
            link(nc.vector.tensor_copy(blk_row, obank[0:1, 0:2 * P]))
            nc.vector.tensor_copy(table[0:1, 0:2 * P], blk_row)
            nc.vector.tensor_tensor(table[0:1, FRESH:FRESH + 2 * P - 1], blk_row[:, 1:2 * P], blk_row[:, 0:2 * P - 1],
                                    ALU.not_equal).then_inc(table_ready, 1)
            dve.wait_ge(table_ready, 1)
            for t in range(5, NT):
                start_sum(t)

            LINKS = 4
            at_link = [0]

            def step(made, i):
                at_link[0] += 1
                made.then_inc(moe_step, 1)
                dve.wait_ge(moe_step, at_link[0] if i is None else 2 * LINKS * i + at_link[0])

            def one_hot(b, e, i):
                step(nc.vector.tensor_scalar(d8[:, :].unsqueeze(1), dest[:, bass.ds(e, 1), :], blk_base[:, b:b + 1], None,
                                             ALU.subtract), i)
                nc.vector.tensor_copy(slot_cols[:, b, :, 3:6],
                                      gparts[:, bass.ds(e, 1), :, :].rearrange("p o t g -> p (o t) g"))
                step(nc.vector.tensor_scalar(blk_base[:, b:b + 1], blk_base[:, b:b + 1], float(EXP_BLOCK), None,
                                             ALU.add), i)
                nc.vector.tensor_tensor(onehot[:, b], iota_s[:, :].unsqueeze(1).broadcast_to([P, NT, P]),
                                        d8[:, :].unsqueeze(2).broadcast_to([P, NT, P]),
                                        ALU.is_equal).then_inc(onehot_ready, 1)

            def frames(b, i):
                got = sbank[:, 8 * b:8 * b + 8]
                nc.vector.tensor_reduce(idx_tmp[:, b, 0:1], got[:, 0:2], AX.X, ALU.add)
                nc.vector.tensor_scalar(idx_tmp[:, b, 1:2], got[:, 2:3], pcol[:, 1:2], pcol[:, 2:3],
                                        ALU.mult, ALU.add)
                step(nc.vector.tensor_reduce(gate_new[:, b:b + 1], got[:, 3:6], AX.X, ALU.add), i)
                nc.vector.tensor_tensor(idx_new[:, b:b + 1], idx_tmp[:, b, 0:1], idx_tmp[:, b, 1:2],
                                        ALU.add).then_inc(idx_ready, 1)

            def split_rows(b, count):
                for n in range(2):
                    dve.wait_ge(xt_rounded, count + n + 1)
                    nc.vector.tensor_tensor(xgT_lo[:, b, 4 * n:4 * n + 4, :],
                                            ptb[n].rearrange("p (k r) -> p k r", k=4),
                                            xgT_hi[:, b, 4 * n:4 * n + 4, :].bitcast(F32),
                                            ALU.subtract).then_inc(xt_copied, 1)

            def split_weights(b, first, parts):
                for q in parts:
                    dve.wait_ge(gu_rounded, first + q + 1)
                    nc.vector.tensor_tensor(gu_lo[b][:, 2 * q:2 * q + 2, :], gu_w[b][:, 2 * q:2 * q + 2, :],
                                            gu_hi[b][:, 2 * q:2 * q + 2, :].bitcast(F32),
                                            ALU.subtract).then_inc(gu_split, 1)

            for j in range(3):
                at = STREAM1 * (j % 2) + j // 2
                e = dve.value_load(table[0:1, at:at + 1], min_val=0, max_val=N_EXP - 1)
                if j == 2:
                    dve.wait_ge(idx_full, 1)
                one_hot(j % 2, e, None)
                if j < 2:
                    dve.wait_ge(idx_full, j + 1)
                    frames(j, None)
            dve.wait_ge(acc_stored, 16 * NT)
            split_weights(0, 0, range(GU_PARTS))
            split_rows(0, 0)
            turns = dve.value_load(table[0:1, TURNS:TURNS + 1], min_val=1, max_val=MAX_TURNS)
            with dve.Fori(0, turns) as i:
                for b in range(2):
                    dve.wait_ge(idx_ready, 2 * i + b + 1)
                    dve.wait_ge(scattered, 32 * i + 16 * b + 16)
                    nc.vector.tensor_copy(idx_now[:, b:b + 1], idx_new[:, b:b + 1])
                    step(nc.vector.tensor_copy(gate_now[:, b:b + 1], gate_new[:, b:b + 1]), i)
                    e = dve.value_load(table[0:1, bass.ds(i + 1 + b + STREAM1 * (1 - b), 1)], min_val=0, max_val=N_EXP - 1)
                    dve.wait_ge(idx_full, 2 * i + b + 2)
                    one_hot(1 - b, e, i)
                    split_weights(1 - b, 2 * GU_PARTS * i + GU_PARTS * (b + 1), range(0, V_SPLIT))
                    dve.wait_ge(silu_done, 2 * i + b + 1)
                    nc.vector.scalar_tensor_tensor(h_exp[:, b, :], h_exp[:, b, :], gate_now[:, b:b + 1],
                                                   wide[0][:, HALF * b + D_EXP:HALF * b + 2 * D_EXP],
                                                   ALU.mult, ALU.mult).then_inc(h_ready, 1)
                    dve.wait_ge(ht_full, 2 * i + b + 1)
                    nc.vector.tensor_copy(hT_exp[:, b], obank[:, 256 * b:256 * b + 256]
                                          .rearrange("p (k r) -> p k r", k=2)).then_inc(ht_copied, 1)
                    split_rows(1 - b, 4 * i + 2 * b + 2)
                    dve.wait_ge(idx_full, 2 * i + b + 3)
                    frames(b, i)
                    split_weights(1 - b, 2 * GU_PARTS * i + GU_PARTS * (b + 1), range(V_SPLIT, GU_PARTS))
            x = xnorm["3"]
            dve.wait_ge(gb_loaded, 128)
            for t in range(NT + 2):
                if t < NT:
                    dve.wait_ge(x_loaded[t], 64)
                    for h in range(2):
                        last = nc.vector.bn_stats(stats[:, t, h, :], x[:, t, HALF * h:HALF * h + HALF])
                    link(last)
                    nc.vector.bn_aggr(mv[:, t, :], stats[:, t, :, :]).then_inc(ln_stat, 1)
                if t >= 2:
                    u = t - 2
                    dve.wait_ge(out_norm, u + 1)
                    nc.vector.tensor_tensor(x[:, u, :], x[:, u, :], gb[:, 0:U], ALU.mult).then_inc(ln_done, 1)
                if 1 <= t <= NT:
                    u = t - 1
                    dve.wait_ge(ln_std, NT * 3 + u + 1)
                    link(nc.vector.reciprocal(rstd[:, u:u + 1], rstd[:, u:u + 1]))
                    nc.vector.scalar_tensor_tensor(nbias[:, u:u + 1], mv[:, u, 0:1], -1.0, rstd[:, u:u + 1],
                                                   ALU.mult, ALU.mult).then_inc(out_scale, 1)


def kernel(**inputs):
    import numpy as _np
    import concourse.bacc as _bacc
    from concourse.bass_utils import run_bass_kernel_spmd as _run

    nc = _bacc.Bacc("TRN2", target_bir_lowering=False, num_devices=1)
    arrays, ins = {}, {}
    for name, value in inputs.items():
        a = _np.ascontiguousarray(value)
        arrays[f"in_{name}"] = a
        ins[name] = nc.dram_tensor(f"in_{name}", a.shape, mybir.dt.from_np(a.dtype), kind="ExternalInput").ap()
    out = nc.dram_tensor("out_h", (1, S, D), F32, kind="ExternalOutput").ap()
    h_res = nc.dram_tensor("h_res", (S, D), F32, kind="Internal").ap()
    h_table = nc.dram_tensor("h_table", (S + P, D), F32, kind="Internal").ap()
    acc = nc.dram_tensor("acc", (S + P, D), F32, kind="Internal").ap()
    build(nc, ins, out, h_res, h_table, acc)
    r = _run(nc, [arrays], core_ids=[0])
    return r.results[0]["out_h"]
```
